# Optimizing a Trainium2 kernel written in Bass

```python
import math
import jax, jax.numpy as jnp
from jax import lax
import numpy as np

D_MODEL = 2048
BATCH = 1
SEQ = 256
DEPTH = 1

GRID_W = 64
CTX_LEN = 256
D_SSM = 1024
GROUP_CH = 16
SSM_GROUPS = D_SSM // GROUP_CH
SSM_STATE = 64
N_DIR = 2
DT_MIN = 1e-3
DT_MAX = 1e-1
N_HEADS = 8
HEAD_DIM = 64
V_DIM = 2 * HEAD_DIM
D_QK = N_HEADS * 2 * HEAD_DIM
D_ATTN = N_HEADS * V_DIM
ATTN_SCALE = HEAD_DIM ** -0.5
ROPE_AXIS_DIM = HEAD_DIM // 2
ROPE_BASE = 10000.0
Q_BLOCK = 128
D_FF = ((8 * D_MODEL + 3 * 256 - 1) // (3 * 256)) * 256
D_IN = D_SSM + 2 * D_QK + D_ATTN + 2 * D_MODEL
IN_SPLITS = (D_SSM, D_SSM + D_QK, D_SSM + 2 * D_QK, D_SSM + 2 * D_QK + D_ATTN,
             D_SSM + 2 * D_QK + D_ATTN + D_MODEL)
EPS = 1e-6

kernel_name = "hybrid_s5_diffattn_dit_block"

def rms_norm(x, g):
    xf = x.astype(jnp.float32)
    y = xf * lax.rsqrt(jnp.mean(xf * xf, axis=-1, keepdims=True) + EPS)
    return (y * g.astype(jnp.float32)).astype(x.dtype)

def modulate(h, shift, scale):
    return h * (1.0 + scale) + shift

def axial_rope_tables(rows):
    row = jnp.repeat(jnp.arange(rows, dtype=jnp.float32), GRID_W)
    col = jnp.tile(jnp.arange(GRID_W, dtype=jnp.float32), rows)
    inv = 1.0 / (ROPE_BASE ** (jnp.arange(0, ROPE_AXIS_DIM, 2, dtype=jnp.float32) / ROPE_AXIS_DIM))
    ang_r = (row[:, None] * inv)[:, None, None, :]
    ang_c = (col[:, None] * inv)[:, None, None, :]
    return jnp.cos(ang_r), jnp.sin(ang_r), jnp.cos(ang_c), jnp.sin(ang_c)

def rope_half(x, cos, sin):
    x1, x2 = jnp.split(x, 2, axis=-1)
    return jnp.concatenate([x1 * cos - x2 * sin, x2 * cos + x1 * sin], axis=-1)

def apply_axial_rope(x, tables):
    cos_r, sin_r, cos_c, sin_c = tables
    xr, xc = jnp.split(x.astype(jnp.float32), 2, axis=-1)
    out = jnp.concatenate([rope_half(xr, cos_r, sin_r), rope_half(xc, cos_c, sin_c)], axis=-1)
    return out.astype(x.dtype)

def s5_discretise(a_re, a_im, log_dt, b_re, b_im):
    lam = lax.complex(a_re.astype(jnp.float32), a_im.astype(jnp.float32))
    dt = jnp.exp(log_dt.astype(jnp.float32))[:, None]
    lam_bar = jnp.exp(lam * dt)
    b = lax.complex(b_re.astype(jnp.float32), b_im.astype(jnp.float32))
    b_bar = ((lam_bar - 1.0) / lam)[..., None] * b
    return lam_bar, b_bar

def linear_scan(lam_bar, bu):
    a = jnp.broadcast_to(lam_bar, (1, bu.shape[1]) + lam_bar.shape)

    def combine(e1, e2):
        a1, b1 = e1
        a2, b2 = e2
        return a2 * a1, a2 * b1 + b2

    _, states = lax.associative_scan(combine, (a, bu), axis=1)
    return states

def s5_glu(y, w_glu, b_glu, dtype):
    z = jax.nn.gelu(y)
    return (z * jax.nn.sigmoid(z @ w_glu + b_glu)).astype(dtype)

def s5_branch(u_c, u_l, a_re, a_im, log_dt, b_re, b_im, c_re, c_im, d_skip, w_glu, b_glu, with_ctx):
    bsz, lc, _ = u_c.shape
    n_lat = u_l.shape[1]
    uc = u_c.astype(jnp.float32).reshape(bsz, lc, SSM_GROUPS, GROUP_CH)
    ul = u_l.astype(jnp.float32).reshape(bsz, n_lat, SSM_GROUPS, GROUP_CH)
    ys_c, ys_l = [], []
    for direction in range(N_DIR):
        rev = direction == 1
        lam_bar, b_bar = s5_discretise(a_re[direction], a_im[direction], log_dt[direction],
                                       b_re[direction], b_im[direction])
        c_mat = lax.complex(c_re[direction].astype(jnp.float32), c_im[direction].astype(jnp.float32))
        uc_d = jnp.flip(uc, axis=1) if rev else uc
        ul_d = jnp.flip(ul, axis=1) if rev else ul
        bu_c = jnp.einsum('blgc,gpc->blgp', uc_d.astype(jnp.complex64), b_bar)
        st_c = linear_scan(lam_bar, bu_c)
        bu_l = jnp.einsum('blgc,gpc->blgp', ul_d.astype(jnp.complex64), b_bar)
        bu_l = bu_l.at[:, 0].add(lam_bar * st_c[:, -1])
        st_l = linear_scan(lam_bar, bu_l)
        yl = jnp.real(jnp.einsum('blgp,gcp->blgc', st_l, c_mat))
        ys_l.append(jnp.flip(yl, axis=1) if rev else yl)
        if with_ctx:
            yc = jnp.real(jnp.einsum('blgp,gcp->blgc', st_c, c_mat))
            ys_c.append(jnp.flip(yc, axis=1) if rev else yc)
    d = d_skip.astype(jnp.float32).reshape(SSM_GROUPS, GROUP_CH)
    y_l = (ys_l[0] + ys_l[1] + d * ul).reshape(bsz, n_lat, D_SSM)
    y_l = s5_glu(y_l, w_glu, b_glu, u_l.dtype)
    y_c = None
    if with_ctx:
        y_c = (ys_c[0] + ys_c[1] + d * uc).reshape(bsz, lc, D_SSM)
        y_c = s5_glu(y_c, w_glu, b_glu, u_c.dtype)
    return y_c, y_l

def diff_attention(q, k, v, lam):
    s = jnp.einsum('bqhmd,bkhmd->bhmqk', q, k).astype(jnp.float32) * ATTN_SCALE
    p = jax.nn.softmax(s, axis=-1)
    p = p[:, :, 0] - lam * p[:, :, 1]
    return jnp.einsum('bhqk,bkhe->bqhe', p.astype(v.dtype), v)

def blocked_diff_attention(q, k, v, lam):
    bsz, n_lat, heads = q.shape[:3]
    nb = n_lat // Q_BLOCK
    qb = jnp.moveaxis(q.reshape(bsz, nb, Q_BLOCK, heads, 2, HEAD_DIM), 1, 0)
    ob = lax.map(lambda blk: diff_attention(blk, k, v, lam), qb)
    return jnp.moveaxis(ob, 0, 1).reshape(bsz, n_lat, heads, V_DIM)

def head_out(o, g, lam_init):
    return (rms_norm(o, g) * (1.0 - lam_init)).reshape(o.shape[0], o.shape[1], D_ATTN)

def branch_merge(y_ssm, o_attn, g_s, g_a, w_ps, w_pa, w_o):
    merged = jax.nn.sigmoid(g_s) * (y_ssm @ w_ps) + jax.nn.sigmoid(g_a) * (o_attn @ w_pa)
    return merged @ w_o

def swiglu(h, w_in, w_out):
    gate, up = jnp.split(h @ w_in, 2, axis=-1)
    return (jax.nn.silu(gate) * up) @ w_out

def setup_inputs(seed: int = 0) -> dict:
    key = jax.random.key(seed)
    ks = jax.random.split(key, 32)
    f32 = jnp.float32

    def nrm(k, shape, s):
        return jax.random.normal(k, shape, f32) * s

    ssm_shape = (DEPTH, N_DIR, SSM_GROUPS, SSM_STATE)
    return {
        "x": nrm(ks[0], (BATCH, SEQ, D_MODEL), 1.0),
        "c": nrm(ks[1], (BATCH, D_MODEL), 1.0),
        "ctx": nrm(ks[2], (BATCH, CTX_LEN, D_MODEL), 1.0),
        "c_ctx": nrm(ks[3], (D_MODEL,), 1.0),
        "w_ada": nrm(ks[4], (DEPTH, D_MODEL, 6 * D_MODEL), 0.5 * D_MODEL ** -0.5),
        "b_ada": nrm(ks[5], (DEPTH, 6 * D_MODEL), 0.02),
        "norm1_g": 1.0 + nrm(ks[6], (DEPTH, D_MODEL), 0.02),
        "w_in": nrm(ks[7], (DEPTH, D_MODEL, D_IN), D_MODEL ** -0.5),
        "ssm_a_re": -0.5 + nrm(ks[8], ssm_shape, 0.01),
        "ssm_a_im": jnp.pi * jnp.arange(SSM_STATE, dtype=f32) + nrm(ks[9], ssm_shape, 0.01),
        "ssm_log_dt": jax.random.uniform(ks[10], (DEPTH, N_DIR, SSM_GROUPS), f32,
                                         math.log(DT_MIN), math.log(DT_MAX)),
        "ssm_b_re": nrm(ks[11], ssm_shape + (GROUP_CH,), (2 * GROUP_CH) ** -0.5),
        "ssm_b_im": nrm(ks[12], ssm_shape + (GROUP_CH,), (2 * GROUP_CH) ** -0.5),
        "ssm_c_re": nrm(ks[13], (DEPTH, N_DIR, SSM_GROUPS, GROUP_CH, SSM_STATE), (2 * SSM_STATE) ** -0.5),
        "ssm_c_im": nrm(ks[14], (DEPTH, N_DIR, SSM_GROUPS, GROUP_CH, SSM_STATE), (2 * SSM_STATE) ** -0.5),
        "ssm_d": nrm(ks[15], (DEPTH, D_SSM), 1.0),
        "w_glu": nrm(ks[16], (DEPTH, D_SSM, D_SSM), D_SSM ** -0.5),
        "b_glu": nrm(ks[17], (DEPTH, D_SSM), 0.02),
        "lambda_q1": nrm(ks[18], (DEPTH, HEAD_DIM), 0.1),
        "lambda_k1": nrm(ks[19], (DEPTH, HEAD_DIM), 0.1),
        "lambda_q2": nrm(ks[20], (DEPTH, HEAD_DIM), 0.1),
        "lambda_k2": nrm(ks[21], (DEPTH, HEAD_DIM), 0.1),
        "subln_g": 1.0 + nrm(ks[22], (DEPTH, V_DIM), 0.02),
        "w_proj_ssm": nrm(ks[23], (DEPTH, D_SSM, D_MODEL), D_SSM ** -0.5),
        "w_proj_attn": nrm(ks[24], (DEPTH, D_ATTN, D_MODEL), D_ATTN ** -0.5),
        "w_out": nrm(ks[25], (DEPTH, D_MODEL, D_MODEL), D_MODEL ** -0.5),
        "norm2_g": 1.0 + nrm(ks[26], (DEPTH, D_MODEL), 0.02),
        "w_ffn_in": nrm(ks[27], (DEPTH, D_MODEL, 2 * D_FF), D_MODEL ** -0.5),
        "w_ffn_out": nrm(ks[28], (DEPTH, D_FF, D_MODEL), D_FF ** -0.5),
        "norm_f_g": 1.0 + nrm(ks[29], (D_MODEL,), 0.02),
    }

def reference(x, c, ctx, c_ctx, w_ada, b_ada, norm1_g, w_in, ssm_a_re, ssm_a_im, ssm_log_dt,
              ssm_b_re, ssm_b_im, ssm_c_re, ssm_c_im, ssm_d, w_glu, b_glu,
              lambda_q1, lambda_k1, lambda_q2, lambda_k2, subln_g,
              w_proj_ssm, w_proj_attn, w_out, norm2_g, w_ffn_in, w_ffn_out, norm_f_g):
    bsz, n_lat, _ = x.shape
    n_ctx = ctx.shape[1]
    rows = n_lat // GRID_W
    rope = axial_rope_tables(rows)
    silu_c = jax.nn.silu(c)
    silu_cc = jax.nn.silu(c_ctx)

    for li in range(DEPTH):
        with_ctx = li < DEPTH - 1
        lam_init = 0.8 - 0.6 * math.exp(-0.3 * li)
        mod = silu_c @ w_ada[li] + b_ada[li]
        mod_c = silu_cc @ w_ada[li] + b_ada[li]
        sh1, sc1, g1, sh2, sc2, g2 = jnp.split(mod[:, None, :], 6, axis=-1)
        sh1c, sc1c, g1c, sh2c, sc2c, g2c = jnp.split(mod_c, 6, axis=-1)

        h = modulate(rms_norm(x, norm1_g[li]), sh1, sc1)
        hc = modulate(rms_norm(ctx, norm1_g[li]), sh1c, sc1c)
        u, q, k, v, g_s, g_a = jnp.split(h @ w_in[li], IN_SPLITS, axis=-1)
        uc, qc, kc, vc, g_sc, g_ac = jnp.split(hc @ w_in[li], IN_SPLITS, axis=-1)

        y_ssm_c, y_ssm = s5_branch(uc, u, ssm_a_re[li], ssm_a_im[li], ssm_log_dt[li],
                                   ssm_b_re[li], ssm_b_im[li], ssm_c_re[li], ssm_c_im[li],
                                   ssm_d[li], w_glu[li], b_glu[li], with_ctx)

        lq1 = lambda_q1[li].astype(jnp.float32)
        lk1 = lambda_k1[li].astype(jnp.float32)
        lq2 = lambda_q2[li].astype(jnp.float32)
        lk2 = lambda_k2[li].astype(jnp.float32)
        lam = jnp.exp(jnp.sum(lq1 * lk1)) - jnp.exp(jnp.sum(lq2 * lk2)) + lam_init
        q = apply_axial_rope(q.reshape(bsz, n_lat, N_HEADS, 2, HEAD_DIM), rope)
        k = apply_axial_rope(k.reshape(bsz, n_lat, N_HEADS, 2, HEAD_DIM), rope)
        v = v.reshape(bsz, n_lat, N_HEADS, V_DIM)
        kc = kc.reshape(bsz, n_ctx, N_HEADS, 2, HEAD_DIM)
        vc = vc.reshape(bsz, n_ctx, N_HEADS, V_DIM)
        k_all = jnp.concatenate([k, kc], axis=1)
        v_all = jnp.concatenate([v, vc], axis=1)
        o = head_out(blocked_diff_attention(q, k_all, v_all, lam), subln_g[li], lam_init)

        x_mid = x + g1 * branch_merge(y_ssm, o, g_s, g_a, w_proj_ssm[li], w_proj_attn[li], w_out[li])

        if with_ctx:
            oc = diff_attention(qc.reshape(bsz, n_ctx, N_HEADS, 2, HEAD_DIM), kc, vc, lam)
            oc = head_out(oc, subln_g[li], lam_init)
            ctx = ctx + g1c * branch_merge(y_ssm_c, oc, g_sc, g_ac, w_proj_ssm[li],
                                           w_proj_attn[li], w_out[li])
            ctx = ctx + g2c * swiglu(modulate(rms_norm(ctx, norm2_g[li]), sh2c, sc2c),
                                     w_ffn_in[li], w_ffn_out[li])

        x = x_mid + g2 * swiglu(modulate(rms_norm(x_mid, norm2_g[li]), sh2, sc2),
                                w_ffn_in[li], w_ffn_out[li])

    return rms_norm(x, norm_f_g)


_drawn_inputs = setup_inputs


def setup_inputs(seed=0):
    import zlib

    import numpy as np

    out = dict(_drawn_inputs(seed))
    spreads = {}
    factors = {'norm1_g': 8.0,
     'ssm_a_re': 64.0,
     'ssm_a_im': 64.0,
     'ssm_log_dt': 64.0,
     'ssm_b_re': 64.0,
     'ssm_b_im': 64.0,
     'ssm_c_re': 64.0,
     'ssm_c_im': 64.0,
     'b_glu': 30.455,
     'lambda_q1': 3.589,
     'lambda_q2': 8.0,
     'lambda_k2': 8.0,
     'subln_g': 26.156,
     'norm2_g': 8.0,
     'norm_f_g': 8.034}
    for name, (base, spread) in spreads.items():
        noise = np.random.default_rng([zlib.crc32(name.encode()), seed]).standard_normal(out[name].shape)
        drawn = base * np.exp(spread * noise) if base else spread * noise
        out[name] = __import__('jax').numpy.asarray(drawn.astype(out[name].dtype))
    for name, factor in factors.items():
        out[name] = (out[name] * factor).astype(out[name].dtype)
    return out
```

```python
from contextlib import ExitStack, contextmanager

import numpy as np

import concourse.bass as bass
from concourse import mybir

ALU = mybir.AluOpType
ACT = mybir.ActivationFunctionType
F32 = mybir.dt.float32
F32R = mybir.dt.float32r
I32 = mybir.dt.int32
AX_X = mybir.AxisListType.X
ds = bass.ds

P = 128
D = 2048
KT = D // P
L = 256
TT = L // P
NB = 512
SSM, G, GC, NS = 1024, 64, 16, 64
CH = 8
NCH = L // CH
H, HD = 8, 64
SCALE = HD ** -0.5
FF = 5632
FB = FF // NB
FK = FF // P
EPS = 1e-6
LAM_INIT = 0.8 - 0.6
NQ = G // 4
KB = 1024

TWO_PI_PARTS = (6.28125, 0.0019350051879882812, 3.019916050561733e-07)
LN2_PARTS = (0.693359375, -2.12194440054690583e-4)
ROUND = 12582912.0
EXP_TAYLOR = [1 / 5040, 1 / 720, 1 / 120, 1 / 24, 1 / 6, 1 / 2, 1.0]


class Tally:

    def __init__(self, sem, start=0):
        self.sem, self.base, self.i, self.per, self.n = sem, start, None, 0, 0

    def tick(self, ins):
        self.n += 1
        return ins.then_inc(self.sem, 1)

    def value(self):
        v = self.base + self.n
        return v if self.i is None else self.i * self.per + v

    def wait(self, eng):
        eng.wait_ge(self.sem, self.value())


@contextmanager
def repeat(eng, lo, hi, per):
    with eng.Fori(lo, hi) as i:
        for t, n in per.items():
            t.base += t.n - lo * n
            t.n, t.i, t.per = 0, i, n
        yield i
        for t, n in per.items():
            assert t.n == n, (t.sem, t.n, n)
    for t, n in per.items():
        t.base += hi * n
        t.n, t.i = 0, None


def layer_program(nc, a, out):
    ctx = ExitStack()
    with ctx:
        def small(name, shape, dt=F32):
            return ctx.enter_context(nc.sbuf_tensor(name, shape, dt))

        def sem(name):
            return ctx.enter_context(nc.semaphore(name))

        ident = small("ident", [P, P])
        ones = small("ones", [P, P])
        rope = small("rope", [P, TT, 2, HD])
        vcol = small("vcol", [P, 112])
        vcol1 = small("vcol1", [P, 57])
        silu_c = small("silu_c", [P, KT, 2])
        mod1 = small("mod1", [P, 2 * KT, 2])
        gain1 = small("gain1", [P, KT, 2])
        modraw = small("modraw", [P, 64])
        modc = small("modc", [P, 64])
        gain2 = small("gain2", [P, KT])
        lam_t = small("lam_t", [P, 3, G])
        lam8_t = small("lam8_t", [P, 3, G])
        dskip = small("dskip", [GC, G])
        ss = small("ss", [P, 4])
        rstd = small("rstd", [P, 4])
        neg_lam = small("neg_lam", [P, 4])
        row_max = small("row_max", [P, 2, 2])
        neg_max = small("neg_max", [P, 2, 2])
        row_sum = small("row_sum", [P, 2, 2])
        row_inv = small("row_inv", [P, 2, 2])
        oss = small("oss", [P, 2 * H])
        gsub = small("gsub", [P, 1])

        arena = (nc.sbuf_base + 31) // 32 * 32
        top = 202

        def at(name, kib, shape, dt=F32):
            size = int(np.prod(shape[1:])) * 4
            assert kib * KB + size <= top * KB, (name, kib, size)
            return nc.alloc_sbuf_tensor_at(name, shape, dt, offset=arena + int(kib * KB))

        assert arena + top * KB <= nc.sbuf_usable_end, (arena, nc.sbuf_usable_end)
        raw = at("raw", 0, [P, 4, 2, NB])
        wring = at("wring", 16, [P, 4, 2, 2, NB], F32R)
        mod_row = at("mod_row", 16, [P, 8 * NB])
        hT = at("hT", 32, [P, 2, 2, KT, L], F32R)
        xin = at("xin", 96, [P, 4, D])
        xT = at("xT", 128, [P, KT, 2 * L])
        square = at("square", 160, [P, D])
        bbar = at("bbar", 170, [P, 2, G, GC])
        tab = at("tab", 178, [P, 2, G, CH])
        braw = at("braw", 182, [P, 2, G, GC])
        btmp = at("btmp", 190, [P, G, GC])
        pw = at("pw", 194, [P, 9, 2, G])
        vrows = at("vrows", 200, [P, 2, P])
        lam_in = at("lam_in", 168, [P, 4, HD])
        lam_pr = at("lam_pr", 169, [P, 2, HD])
        par = at("par", 32, [P, 24, G])
        par_i = at("par_i", 40, [P, G], I32)
        par_in = at("par_in", 42, [P, 2, P])
        ustate = at("ustate", 96, [P, 2 * NCH, 2, G])
        uT = at("uT", 128, [P, 8, 2 * L])
        u = at("u", 128, [P, G, 2 * NCH])
        kT = at("kT", 144, [P, H, 2 * L])
        kraw = at("kraw", 160, [P, 4, NB])
        half_t = at("half_t", 168, [P, NB])
        u_s = at("u_s", 168, [P, CH, 2 * NCH])
        gp = at("gp", 182, [P, 2, 2, 4, P])
        ptmp = [at("ptmp0", 190, [P, NB]), at("ptmp1", 200, [P, NB])]
        gt = at("gt", 192, [P, 2, 4, P])
        uv = at("uv", 192, [P, 8, CH, GC])
        acc = at("acc", 196, [P, 2, NB])
        scan_t = at("scan_t", 190, [P, 2, 2, G])
        v = at("v", 48, [P, 4, SSM])
        qraw = at("qraw", 182, [P, 2, NB])
        qT = at("qT", 192, [P, H, L])
        qh = at("qh", 164, [P, 2, L])
        o_all = at("o_all", 192, [P, H, 2, P])
        prob = at("prob", 182, [P, 2, 2, NB])
        pT = at("pT", 160, [P, 2, 4, P])
        gate_st = at("gate_st", 166, [P, NB])
        osq = at("osq", 182, [P, 2 * H, P])
        oT = at("oT", 48, [P, 2, H, L], F32R)
        c_in = at("c_in", 144, [P, 2, 8, P])
        cT = at("cT", 96, [P, 2, G, GC])
        strip_r = at("strip_r", 104, [P, 2, 4, 15, GC])
        rmat = at("rmat", 182, [P, 2, 2, 4, CH, GC])
        rtmp = [at("rtmp0", 190, [P, NB]), at("rtmp1", 168, [P, NB])]
        strip = at("strip", 144, [GC, 2, 4, 15 * GC])
        toep = at("toep", 152, [P, 2, 4, P])
        hq = at("hq", 156, [P, 2, 2, 4, NCH])
        hq_raw = at("hq_raw", 158, [P, 2, 4, NCH])
        hq_t = at("hq_t", 159, [P, 2, 4, NCH])
        yj = at("yj", 160, [NCH, CH, P])
        dblk = at("dblk", 151.5, [GC, 4, GC])
        bquad = at("bquad", 164, [P, 2, 2, 4, GC])
        uquad = at("uquad", 165, [P, 2, 4, NCH])
        z = at("z", 192, [P, 8, L])
        zs = at("zs", 96, [P, 2, 8, L], F32R)
        sig = at("sig", 168, [P, 4, L])
        y32 = at("y32", 172, [P, 4, L])
        ys = at("ys", 112, [P, 2, 8, L], F32R)
        diag = at("diag", 144, [P, 16, P])
        g1row = at("g1row", 176, [P, D])
        gates = at("gates", 64, [P, 4, 2, TT, NB])
        m_ssm = at("m_ssm", 168, [P, TT, NB])
        merged = at("merged", 172, [P, TT, NB])
        mT = at("mT", 128, [P, 2, KT, L], F32R)
        x = at("x", 186, [P, TT, D])
        gx = at("gx", 160, [P, TT, NB])
        x2 = at("x2", 96, [P, TT, D])
        square2 = at("square2", 112, [P, D])
        h32 = at("h32", 128, [P, KT, L])
        h2T = at("h2T", 64, [P, 2, KT, L], F32R)
        silu_g = at("silu_g", 48, [P, TT, NB])
        act32 = at("act32", 52, [P, TT, NB])
        g2row = at("g2row", 56, [P, D])
        acc2 = at("acc2", 200, [P, NB])
        actT = at("actT", 96, [P, 2, FK, L], F32R)
        diag2 = at("diag2", 64, [P, 16, P])
        act_s = at("act_s", 64, [P, 2, 2, 2, L], F32R)
        normf = at("normf", 72, [P, D])
        fin = at("fin", 96, [P, TT, D])
        gx_f = at("gx_f", 48, [P, TT, NB])
        square3 = at("square3", 80, [P, D])

        ps = ctx.enter_context(nc.psum_tensor("ps", [P, 8, NB], F32))

        v_spill = nc.dram_tensor("v_spill", [2 * L, SSM], F32, kind="Internal").ap()
        g_spill = nc.dram_tensor("g_spill", [8, L, NB], F32, kind="Internal").ap()

        raw_landed = [sem(f"raw_landed{s}") for s in range(4)]
        s_consts, s_vecs, s_params, s_braw, s_lams = (sem(n) for n in ("consts", "vecs", "params", "braw_in", "lams_in"))
        s_x, s_spill, s_v, s_cin, s_xre, s_normf, s_out = (
            sem(n) for n in ("x_in", "v_spilled", "v_back", "c_landed", "x_again", "normf_in", "out_stored"))
        s_toep = [sem("toep_landed0"), sem("toep_landed1")]
        ada_used = sem("ada_used")
        ada2_used = sem("ada2_used")
        hi_done, lo_done = sem("hi_done"), sem("lo_done")
        mm_done = sem("mm_done")
        main_free = sem("main_free")
        ada_cols = sem("ada_cols")
        mod_out = sem("mod_out")
        pe_misc = sem("pe_misc")
        dve_misc = sem("dve_misc")
        act_misc = sem("act_misc")
        s_ssq, s_sqrt = sem("ssq"), sem("rms_root")
        xT_mm, xT_out = sem("xT_transposed"), sem("xT_copied")
        gains, h_ready, h_hi, h_lo = sem("gains"), sem("h_ready"), sem("h_hi"), sem("h_lo")
        s_sin_in, s_sin = sem("angles"), sem("sines")
        tab_done = sem("tab_done")
        u_sorted, uv_mm, uv_out, u_mm, u_out = (sem(n) for n in ("u_sorted", "uv_mm", "uv_out", "u_mm", "u_out"))
        k_out, k_rot, k_mm, kT_out = (sem(n) for n in ("k_out", "k_rot", "k_mm", "kT_out"))
        g_built, g_mm, g_out, e_mm, e_out = (sem(n) for n in ("g_built", "g_mm", "g_out", "e_mm", "e_out"))
        scanned = sem("scanned")
        q_out, q_rot, q_mm, qT_out = (sem(n) for n in ("q_out", "q_rot", "q_mm", "qT_out"))
        qh_in = sem("qh_in")
        s_mm, s_nm, s_exp, s_pd, t_mm, pT_out, o_mm, o_out = (
            sem(n) for n in ("scores", "neg_max_done", "probs", "pdiff_done", "p_transposed", "pT_out", "o_mm", "o_out"))
        o_norm, oT_mm, oT_hi, oT_lo = (sem(n) for n in ("o_norm", "oT_mm", "oT_hi", "oT_lo"))
        o_ss, o_root = sem("o_ss"), sem("o_root")
        c_mm, c_out = sem("c_mm"), sem("c_out")
        r_built, sr_done, st_mm, st_out, st_done, hq_done, y_mm, yj_out, yT_mm, z_out = (
            sem(n) for n in ("r_built", "strip_r_done", "strip_mm", "strip_copied", "strip_done", "hq_done", "y_mm",
                             "yj_out", "yT_mm", "z_out"))
        zs_hi, zs_lo, glu_sig, glu_y, ys_hi, ys_lo = (
            sem(n) for n in ("zs_hi", "zs_lo", "glu_sig", "glu_y", "ys_hi", "ys_lo"))
        diag_done, row_mm, row_out = sem("diag_done"), sem("row_mm"), sem("row_out")
        gate_sig, ms_done, m_done, mt_mm, mt_hi, mt_lo = (
            sem(n) for n in ("gate_sig", "ms_done", "m_done", "mt_mm", "mt_hi", "mt_lo"))
        s_gspill, s_gates = sem("gates_spilled"), sem("gates_back")
        wo_out, x2_done, x2_mm, h32_done, h2_hi, h2_lo = (
            sem(n) for n in ("wo_out", "x2_done", "x2_mm", "h32_done", "h2_hi", "h2_lo"))
        silu_out, act_done, at_mm, at_hi, at_lo = (sem(n) for n in ("silu_out", "act_done", "at_mm", "at_hi", "at_lo"))
        act_in = sem("act_in")
        ff_out, f_done = sem("ff_out"), sem("f_done")
        dve_seq, act_seq, pool_seq = sem("dve_seq"), sem("act_seq"), sem("pool_seq")

        def tiles(w):
            return w.rearrange("(g k p) (b n) -> g b p k n", k=2, p=P, n=NB)

        ada_v, win_v = tiles(a["w_ada"][0]), tiles(a["w_in"][0])
        glu_v, ps_v, pa_v = tiles(a["w_glu"][0]), tiles(a["w_proj_ssm"][0]), tiles(a["w_proj_attn"][0])
        wo_v, fi_v, fo_v = tiles(a["w_out"][0]), tiles(a["w_ffn_in"][0]), tiles(a["w_ffn_out"][0])

        WU, WQ, WK, WV, WGS, WGA = 0, 2, 4, 6, 8, 12
        M_KV, M_Q, M_GATE, M_GY, M_GLU, M_MERGE, M_WO, M_FI = 16, 48, 64, 96, 128, 136, 168, 200
        M_FO = M_FI + 16 * FB
        R_SHIFT1, R_SHIFT2 = 96, 128
        R_GY = M_GY + R_SHIFT1

        def r_parts(s, q, buffer):
            shape = [P, 4, CH, GC]
            powers = [tab[:, c, ds(q * 4, 4), :].unsqueeze(3).broadcast_to(shape) for c in range(2)]
            cs = [cT[:, c, ds(q * 4, 4), :].unsqueeze(2).broadcast_to(shape) for c in range(2)]
            return powers, cs, buffer[:].rearrange("p (g s c) -> p g s c", g=4, s=CH)

        block = ctx.enter_context(nc.Block())

        @block.sync
        def _(sp):
            def load(src, slot, last_use):
                sp.wait_ge(*last_use)
                sp.dma_start(raw[:, slot], src).then_inc(raw_landed[slot], 16)

            def late(m):
                return lo_done, m - 3

            def in_triples(b, pos):
                if pos < 0:
                    b, pos = b - 1, pos + 24
                if isinstance(b, int) and b < 0:
                    return ada_used, 64 - 24 + pos + 1
                n, e = divmod(pos, 3)
                return (ada2_used, b * 16 + (2 * n + e)) if e else (lo_done, b * 8 + (n + 1))

            for n in range(4):
                sp.dma_start(raw[:, n], ada_v[n, 0]).then_inc(raw_landed[n], 16)
            for g in range(4, 8):
                sp.wait_ge(ada_used, g - 3)
                sp.dma_start(raw[:, g % 4], ada_v[g, 0]).then_inc(raw_landed[g % 4], 16)
            with sp.Fori(1, 8) as b:
                for g in range(8):
                    sp.wait_ge(ada_used, b * 8 + (g - 3))
                    sp.dma_start(raw[:, g % 4], ada_v[g, b]).then_inc(raw_landed[g % 4], 16)

            def triple_block(wb, b):
                for pos in range(24):
                    n, e = divmod(pos, 3)
                    t = 2 * n + e - 1
                    load(ada_v[t % 8, b * 2 + (8 + t // 8)] if e else win_v[n, wb], pos % 4, in_triples(b, pos - 4))

            triple_block(WU, 0)
            triple_block(WU + 1, 1)
            with sp.Fori(0, 2) as i:
                triple_block(i + WK, i * 2 + 2)
                triple_block(i + WV, i * 2 + 3)
            for n in range(2):
                for g in range(8):
                    load(win_v[g, WQ + n], g % 4, late(M_Q + 8 * n + g) if n or g >= 4 else in_triples(5, 20 + g))
                if n == 0:
                    sp.wait_ge(mm_done, M_Q)
                    sp.wait_ge(s_spill, 32)
                    sp.dma_start(v[:], v_spill.rearrange("(t p) n -> p t n", p=P)).then_inc(s_v, 16)
            with sp.Fori(0, 4) as n:
                for g in range(8):
                    load(win_v[g, n + WGS], g % 4, late(n * 8 + (M_GATE + g)))
            sp.wait_ge(s_mm, 2 * H)
            for n, name in enumerate(("ssm_c_re", "ssm_c_im")):
                for d in range(2):
                    src = a[name][0, d].rearrange("(t g) c p -> (g c) t p", g=8)
                    sp.dma_start(c_in[:, n, :, d * NS:(d + 1) * NS], src).then_inc(s_cin, 16)

            def gates_y(n, first):
                for j in range(8):
                    if first and j < 2:
                        before = late(M_GY + 2 * j), late(M_GY + 2 * j + 1)
                    else:
                        before = (lo_done, n * 8 + (M_GY + j - 1)), (ada2_used, n * 8 + (96 + j - 1))
                    load(win_v[j, n + WGA], 2 * j % 4, before[0])
                    load(ada_v[j, n + 20], (2 * j + 1) % 4, before[1])

            gates_y(0, True)
            with sp.Fori(1, 4) as n:
                gates_y(n, False)
            for b in range(2):
                for g in range(4):
                    load(glu_v[g, b], g, late(M_GLU + 4 * b + g) if b else
                         ((ada2_used, 96 + 31 + g // 2) if g % 2 else (lo_done, M_GY + 31 + g // 2)))

            sp.wait_ge(mm_done, M_GLU)
            sp.wait_ge(s_gspill, 16 * 16)

            def merge_block(b):
                for k in range(2):
                    src = g_spill[ds(b + 4 * k, 1)].squeeze(0).rearrange("(t p) n -> p t n", p=P)
                    sp.dma_start(gates[:, ds(b, 1), k].squeeze(1), src).then_inc(s_gates, 16)
                for view, m in ((ps_v, 0), (pa_v, 4)):
                    for g in range(4):
                        load(view[g, b], g, late(b * 8 + (M_MERGE + m + g)))

            with sp.Fori(0, 4) as b:
                merge_block(b)
            sp.wait_ge(glu_y, 8)
            sp.dma_start(x[:], a["x"][0].rearrange("(t p) n -> p t n", p=P)).then_inc(s_xre, 16)
            with sp.Fori(0, 4) as b:
                for g in range(8):
                    load(wo_v[g, b], g % 4, late(b * 8 + (M_WO + g)))

            def ff_tile(j, n):
                return fi_v[n % 8, j if n < 8 else j + FB]

            with sp.Fori(0, FB) as j:
                for n in range(16):
                    load(ff_tile(j, n), n % 4, late(j * 16 + (M_FI + n)))
            sp.wait_ge(mm_done, M_FO)
            sp.dma_start(normf[:], a["norm_f_g"].unsqueeze(0).broadcast_to([P, D])).then_inc(s_normf, 16)
            with sp.Fori(0, FB) as j:
                for g in range(2):
                    for cb in range(4):
                        load(fo_v[j * 2 + g, cb], cb, late(j * 8 + (M_FO + 4 * g + cb)))
            for t in range(TT):
                sp.wait_ge(f_done, t + 1)
                sp.dma_start(out[0, t * P:(t + 1) * P, :], fin[:, t]).then_inc(s_out, 16)
            sp.wait_ge(s_out, 16 * TT)

        @block.tensor
        def _(pe):
            mm = nc.tensor.matmul
            misc = Tally(pe_misc)

            def tr(dst, src, k):
                return nc.tensor.transpose(dst, src, ident[0:k, 0:k])

            def turn(dst, src, k):
                return mm(dst, src, ident[0:k, 0:k], start=True, stop=True)

            pe.wait_ge(s_consts, 32)
            pe.wait_ge(s_vecs, 16 * 7)
            misc.tick(tr(ps[:, 0, 0:112], vrows[0:112, 0], 112))
            misc.tick(tr(ps[:, 1, 0:57], vrows[0:57, 1], 57))
            pe.wait_ge(s_params, 16 * 6)
            tr(ps[:, 7, 0:G], par_in[0:G, 0], G)
            misc.tick(tr(ps[:, 7, G:2 * G], par_in[0:G, 1], G))

            def ada_blocks(i):
                for s in range(2):
                    pe.wait_ge(main_free, i * 2 + (s + 1))
                    for g in range(8):
                        pe.wait_ge(raw_landed[g % 4], i * 64 + (32 * s + 16 * (g // 4) + 16))
                        for k in range(2):
                            ins = mm(ps[0:2, s, :], silu_c[:, 2 * g + k], raw[:, g % 4, k], start=(g + k == 0),
                                     stop=(g == 7 and k == 1))
                            if k:
                                ins.then_inc(ada_used, 1)

            pe.wait_ge(act_misc, 1)
            with pe.Fori(0, 2) as i:
                ada_blocks(i)
            pe.wait_ge(x2_done, 4)

            for k in range(KT):
                if k >= 2:
                    pe.wait_ge(xT_out, k - 1)
                for t in range(4):
                    ins = tr(ps[:, 4 + k % 2, t * P:(t + 1) * P], xin[:, t, k * P:(k + 1) * P], P)
                ins.then_inc(xT_mm, 1)
            with pe.Fori(2, 4) as i:
                ada_blocks(i)
            pe.wait_ge(main_free, 10)
            for j in range(2 * KT):
                ins = tr(ps[:, 6, 2 * j:2 * j + 2], mod_row[0:2, j * P:(j + 1) * P], 2)
            ins.then_inc(ada_cols, 1)

            def item(m, slot, body):
                pe.wait_ge(lo_done, m + 1)
                for k in range(2):
                    ins = body(k, wring[:, slot])
                return ins.then_inc(mm_done, 1)

            def tokens(banks, lhs, start, stop, tls):
                def f(k, w):
                    for n, t in enumerate(tls):
                        hi, lo = lhs(0, k, t), lhs(1, k, t)
                        mm(ps[:, banks + n, :], hi, w[:, 0, k], start=start and k == 0, stop=False)
                        mm(ps[:, banks + n, :], hi, w[:, 1, k], start=False, stop=False)
                        ins = mm(ps[:, banks + n, :], lo, w[:, 0, k], start=False, stop=stop and k == 1)
                    return ins
                return f

            def channels(banks, rhs, start, stop, cols):
                def f(k, w):
                    for c in range(4):
                        dst = ps[:, banks + c, 0:cols]
                        wh, wl = w[:, 0, k, c * P:(c + 1) * P], w[:, 1, k, c * P:(c + 1) * P]
                        mm(dst, wh, rhs(0, k), start=start and k == 0, stop=False)
                        mm(dst, wh, rhs(1, k), start=False, stop=False)
                        ins = mm(dst, wl, rhs(0, k), start=False, stop=stop and k == 1)
                    return ins
                return f

            def ada_reduce(b):
                pe.wait_ge(ada2_used, b * 16 + 16)
                for c in range(8):
                    ins = mm(ps[:, 4, c:c + 1], acc[:, c // 4, (c % 4) * P:(c % 4 + 1) * P], ones[:, 0:1],
                             start=True, stop=True)
                ins.then_inc(ada_cols, 1)

            for b in range(2):
                pe.wait_ge(main_free, 10 + 4 * b)
                for it in range(8):
                    if b == 0:
                        pe.wait_ge(h_lo, 2 * it + 2)
                    item(8 * b + it, it % 2,
                         channels(0, lambda hl, k, it=it: hT[:, :, hl, 2 * it + k, :], it == 0, it == 7, 2 * L))
                ada_reduce(b)

            def h_tok(it):
                return lambda hl, k, t: hT[:, t // TT, hl, 2 * it + k, (t % TT) * P:(t % TT + 1) * P]

            with pe.Fori(0, 2) as i:
                pe.wait_ge(main_free, i * 8 + 18)
                for it in range(8):
                    item(i * 16 + (M_KV + it), it % 2, tokens(0, h_tok(it), it == 0, it == 7, range(4)))
                    if it % 2 == 0:
                        pe.wait_ge(u_sorted, i * 4 + (it // 2 + 1))
                        for s in range(CH):
                            ins = turn(ps[0:2 * NCH, 5 + s // 4, (s % 4) * P:(s % 4 + 1) * P], u_s[:, s], P)
                        ins.then_inc(uv_mm, 1)
                    else:
                        pe.wait_ge(uv_out, i * 4 + (it // 2 + 1))
                        pe.wait_ge(*((e_out, i * 8 + 1) if it == 1 else (u_out, i * 4 + it // 2)))
                        for g in range(8):
                            ins = turn(ps[:, 7, g * 64:(g + 1) * 64], uv[0:64, g].rearrange("p s c -> p (s c)"), 64)
                        ins.then_inc(u_mm, 1)
                ada_reduce(i * 2 + 2)
                pe.wait_ge(main_free, i * 8 + 22)
                for it in range(8):
                    def quad(it=it):
                        pe.wait_ge(g_built, i * 8 + (it + 1))
                        if it == 0:
                            pe.wait_ge(u_out, i * 4 + 4)
                        for c in range(2):
                            for g in range(4):
                                ins = tr(ps[:, 5 + c, g * P:(g + 1) * P], gp[:, it % 2, c, g, :], P)
                        ins.then_inc(g_mm, 1)

                    prods = tokens(0, h_tok(it), it == 0, it == 7, range(4))
                    m = i * 16 + (M_KV + 8 + it)
                    pe.wait_ge(lo_done, m + 1)
                    prods(0, wring[:, it % 2])
                    quad()
                    prods(1, wring[:, it % 2]).then_inc(mm_done, 1)
                    pe.wait_ge(g_out, i * 8 + (it + 1))
                    pe.wait_ge(e_out, i * 8 + (it + 1))
                    for c in range(2):
                        for g in range(4):
                            ins = mm(ps[:, 7, c * 256 + g * 64:c * 256 + (g + 1) * 64], gt[:, c, g, :],
                                     u[:, ds(i * 32 + (4 * it + g), 1), :].squeeze(1), start=True, stop=True)
                    ins.then_inc(e_mm, 1)
                    if 2 <= it < 6:
                        t = it - 2
                        pe.wait_ge(k_rot, i + 1)
                        if t:
                            pe.wait_ge(kT_out, i * 4 + t)
                        for hh in range(4):
                            ins = tr(ps[:, 4, hh * P:(hh + 1) * P], kraw[:, t, hh * P:(hh + 1) * P], P)
                        ins.then_inc(k_mm, 1)
                pe.wait_ge(kT_out, i * 4 + 4)
                ada_reduce(i * 2 + 3)

            def q_transposes(n):
                pe.wait_ge(q_rot, n + 1)
                for t in range(2):
                    for hh in range(4):
                        ins = tr(ps[:, 4 + t, hh * P:(hh + 1) * P], qraw[:, t, hh * P:(hh + 1) * P], P)
                ins.then_inc(q_mm, 1)

            def h_lat(it):
                return lambda hl, k, t: hT[:, 1, hl, 2 * it + k, t * P:(t + 1) * P]

            for n in range(2):
                pe.wait_ge(main_free, 34 + 2 * n)
                for it in range(8):
                    item(M_Q + 8 * n + it, it % 4, tokens(0, h_lat(it), it == 0, it == 7, range(TT)))
                    if n and it == 2:
                        q_transposes(0)
            q_transposes(1)

            def scores(hd, qt):
                for mp in range(2):
                    ins = mm(ps[:, 2 * qt + mp, :], qh[:, mp, qt * P:(qt + 1) * P],
                             kT[:, ds(hd, 1), :].squeeze(1), start=True, stop=True)
                ins.then_inc(s_mm, 1)

            def values(hd, qt, un):
                pe.wait_ge(s_pd, un + 1)
                if not (isinstance(un, int) and un == 0):
                    pe.wait_ge(pT_out, un)
                for t in range(4):
                    ins = tr(ps[:, 4, t * P:(t + 1) * P], prob[:, qt, 0, t * P:(t + 1) * P], P)
                ins.then_inc(t_mm, 1)
                pe.wait_ge(pT_out, un + 1)
                if not (isinstance(un, int) and un == 0):
                    pe.wait_ge(o_out, un)
                for t in range(4):
                    ins = mm(ps[:, 5, qt * P:(qt + 1) * P], pT[:, qt, t, :], v[:, t, ds(hd * P, P)],
                             start=t == 0, stop=t == 3)
                ins.then_inc(o_mm, 1)

            def gate_item(n, k, bank, first):
                if k == 0 and not first:
                    pe.wait_ge(gate_sig, n * 2)
                item(n * 8 + (M_GATE + k), k % 4, tokens(bank, h_lat(k), k == 0, k == 7, range(TT)))

            pe.wait_ge(main_free, 38)
            pe.wait_ge(e_out, NQ + 1)
            pe.wait_ge(qh_in, 1)
            scores(0, 0)
            pe.wait_ge(s_v, 16)

            def att(n, hh, first, last):
                hd = n * 2 + hh
                if not first:
                    pe.wait_ge(s_exp, hd * 2)
                scores(hd, 1)
                gate_item(n, 4 * hh, 6, first)
                values(hd, 0, hd * 2)
                gate_item(n, 4 * hh + 1, 6, first)
                if not last:
                    pe.wait_ge(s_exp, hd * 2 + 1)
                    pe.wait_ge(qh_in, hd + 2)
                    scores(hd + 1, 0)
                gate_item(n, 4 * hh + 2, 6, first)
                values(hd, 1, hd * 2 + 1)
                gate_item(n, 4 * hh + 3, 6, first)

            att(0, 0, True, False)
            att(0, 1, False, False)
            with pe.Fori(1, H // 2 - 1) as n:
                att(n, 0, False, False)
                att(n, 1, False, False)
            att(H // 2 - 1, 0, False, False)
            att(H // 2 - 1, 1, False, True)
            pe.wait_ge(o_norm, 1)
            pe.wait_ge(o_out, 16)
            pe.wait_ge(gate_sig, 8)
            for n in range(4):
                for j in range(4):
                    ins = tr(ps[:, 4 + n, j * P:(j + 1) * P], o_all[:, 2 * n + j // 2, j % 2, :], P)
                ins.then_inc(oT_mm, 1)

            pe.wait_ge(s_cin, 64)
            for n in range(2):
                for c in range(8):
                    ins = tr(ps[:, 2 * n + c // 4, (c % 4) * P:(c % 4 + 1) * P], c_in[:, n, c, :], P)
                ins.then_inc(c_mm, 1)

            def strips(q, s):
                pe.wait_ge(sr_done, q + 1)
                for g in range(4):
                    for c in range(2):
                        ins = mm(ps[0:GC, 6 + g // 2, (g % 2) * 240:(g % 2) * 240 + 240],
                                 bquad[:, s, c, g],
                                 strip_r[:, c, g].rearrange("p b c -> p (b c)"), start=c == 0, stop=c == 1)
                ins.then_inc(st_mm, 1)

            def outputs(q, i, s):
                pe.wait_ge(s_toep[s], i * 128 + 128)
                pe.wait_ge(hq_done, q + 1)
                for g in range(4):
                    dst = ps[0:NCH, 4 + s, g * P:(g + 1) * P]
                    mm(dst, uquad[:, s, g], toep[:, s, g, :], start=True, stop=False)
                    for c in range(2):
                        ins = mm(dst, hq[:, s, c, g, :], rmat[:, s, c, g].rearrange("p t c -> p (t c)"),
                                 start=False, stop=c == 1)
                ins.then_inc(y_mm, 1)

            def y_turn(i):
                pe.wait_ge(yj_out, i * 2 + 2)
                for t in range(CH):
                    ins = turn(ps[:, 0, t * NCH:(t + 1) * NCH], yj[:, t, :], NCH)
                ins.then_inc(yT_mm, 1)

            pe.wait_ge(oT_lo, 4)
            strips(0, 0)

            def y_quad(u, j, first, last):
                i, s = u * 2 + j // 2, j % 2
                q = u * 4 + j
                if not last:
                    pe.wait_ge(st_out, q + 1)
                    strips(q + 1, 1 - s)
                if s == 0 and not first:
                    y_turn(i - 1)
                if not (first or (isinstance(q, int) and q < 2)):
                    pe.wait_ge(yj_out, q - 1)
                outputs(q, i, s)
                for k in range(2):
                    gate_item(u + 4, 2 * j + k, 2, first)

            def y_unit(u, first, last):
                for j in range(4):
                    y_quad(u, j, first and j == 0, last and j == 3)
                pe.wait_ge(ada2_used, u * 8 + (96 + 8))
                pe.wait_ge(mod_out, u + 6)
                for c in range(4):
                    ins = mm(ps[:, 1, c:c + 1], acc2[:, c * P:(c + 1) * P], ones[:, 0:1], start=True, stop=True)
                ins.then_inc(ada_cols, 1)

            pe.wait_ge(c_out, 2)
            y_unit(0, True, False)
            with pe.Fori(1, 3) as unit:
                y_unit(unit, False, False)
            y_unit(3, False, True)
            y_turn(7)

            def rows(src, banks, n, wait_diag):
                pe.wait_ge(diag_done, wait_diag)
                ins = mm(ps[:, banks + n, :], ones[:, :], src, start=True, stop=True)
                ins.then_inc(row_mm, 1)

            pe.wait_ge(yj_out, 16)
            for n in range(4):
                rows(diag[:, 4 * n:4 * n + 4, :].rearrange("p j n -> p (j n)"), 4, n, 1)
            pe.wait_ge(zs_lo, 1)
            pe.wait_ge(z_out, 8)
            for b in range(2):
                if b:
                    pe.wait_ge(row_out, 4)
                for it in range(4):
                    item(M_GLU + 4 * b + it, it, channels(4 * b, lambda hl, k, it=it: zs[:, hl, 2 * it + k, :],
                                                          it == 0, it == 3, L))

            def merge_turn(n):
                pe.wait_ge(m_done, n)
                for c in range(4):
                    for t in range(TT):
                        ins = tr(ps[:, c // 2, (c % 2) * L + t * P:(c % 2) * L + (t + 1) * P],
                                 merged[:, t, c * P:(c + 1) * P], P)
                ins.then_inc(mt_mm, 1)

            def merge(b, first):
                for part, src in ((0, ys), (1, oT)):
                    if first:
                        pe.wait_ge(glu_sig, 8)
                        if part == 0:
                            pe.wait_ge(ys_lo, 2)
                    else:
                        pe.wait_ge(ms_done if part == 0 else m_done, b)
                    for it in range(4):
                        item(b * 8 + (M_MERGE + 4 * part + it), it,
                             tokens(4 + 2 * part, lambda hl, k, t, it=it, src=src: src[:, hl, 2 * it + k, t * P:(t + 1) * P],
                                    it == 0, it == 3, range(TT)))
                        if part == 0 and it == 2 and not first:
                            merge_turn(b)

            merge(0, True)
            with pe.Fori(1, 4) as b:
                merge(b, False)
            merge_turn(4)

            pe.wait_ge(mt_lo, 4)

            def out_proj(i, first):
                for s in range(2):
                    if not first:
                        pe.wait_ge(wo_out, i * 4 - (2 - 2 * s))
                    for it in range(8):
                        item(i * 16 + (M_WO + 8 * s + it), it % 4,
                             tokens(2 * s, lambda hl, k, t, it=it: mT[:, hl, 2 * it + k, t * P:(t + 1) * P],
                                    it == 0, it == 7, range(TT)))

            out_proj(0, True)
            out_proj(1, False)

            pe.wait_ge(m_done, 4)
            for n in range(4):
                rows(diag2[:, 4 * n:4 * n + 4, :].rearrange("p j n -> p (j n)"), 4, n, 2)
            pe.wait_ge(x2_done, 6)
            for n in range(8):
                if n < 4:
                    pe.wait_ge(row_out, 5 + n)
                if n >= 4:
                    pe.wait_ge(h32_done, 2 * (n - 4) + 2)
                for j in range(2):
                    for t in range(TT):
                        ins = tr(ps[:, 4 + n % 4, j * L + t * P:j * L + (t + 1) * P],
                                 x2[:, t, (2 * n + j) * P:(2 * n + j + 1) * P], P)
                ins.then_inc(x2_mm, 1)

            pe.wait_ge(h2_lo, 4)
            pe.wait_ge(wo_out, 8)

            def h2_tok(it):
                return lambda hl, k, t: h2T[:, hl, 2 * it + k, t * P:(t + 1) * P]

            def act_turn(n):
                pe.wait_ge(act_done, n)
                for c in range(4):
                    for t in range(TT):
                        ins = tr(ps[:, 4 + c // 2, (c % 2) * L + t * P:(c % 2) * L + (t + 1) * P],
                                 act32[:, t, c * P:(c + 1) * P], P)
                ins.then_inc(at_mm, 1)

            def ffn_in(j, first):
                m0 = j * 16 + M_FI
                for part in range(2):
                    if not first:
                        pe.wait_ge(*((silu_out, j * 2) if part == 0 else (act_done, j)))
                    for it in range(8):
                        item(m0 + (8 * part + it), it % 4, tokens(2 * part, h2_tok(it), it == 0, it == 7, range(TT)))
                        if part == 0 and it == 2 and not first:
                            act_turn(j)

            ffn_in(0, True)
            with pe.Fori(1, FB) as j:
                ffn_in(j, False)
            act_turn(FB)

            pe.wait_ge(at_lo, FB)
            pe.wait_ge(row_out, 8)

            def ffn_out(j, first, last):
                for g in range(2):
                    for cb in range(4):
                        if cb == 0:
                            pe.wait_ge(act_in, j * 2 + (g + 1))

                        def lhs(hl, k, t, g=g):
                            return act_s[:, g, hl, k, t * P:(t + 1) * P]
                        item(j * 8 + (M_FO + 4 * g + cb), cb,
                             tokens(2 * cb, lhs, first and g == 0, last and g == 1, range(TT)))

            ffn_out(0, True, False)
            with pe.Fori(1, FB - 1) as j:
                ffn_out(j, False, False)
            ffn_out(FB - 1, False, True)

        @block.scalar
        def _(act):
            af = nc.scalar.activation
            seq = Tally(act_seq)

            act.dma_start(ident[:], a["ident"]).then_inc(s_consts, 16)
            act.dma_start(rope[:], a["rope"].rearrange("(t p) s n -> p t s n", p=P)).then_inc(s_consts, 16)
            rows_of = lambda v: v.rearrange("(r p) -> r p", p=P)
            for dst, src in ((vrows[0:96, 0], rows_of(a["b_ada"][0])), (vrows[96:112, 0], rows_of(a["norm1_g"][0])),
                             (vrows[0:16, 1], rows_of(a["norm2_g"][0])), (vrows[16:24, 1], rows_of(a["b_glu"][0])),
                             (vrows[24:25, 1], rows_of(a["subln_g"][0])), (vrows[25:41, 1], rows_of(a["c"][0])),
                             (vrows[41:57, 1], rows_of(a["c_ctx"]))):
                act.dma_start(dst, src).then_inc(s_vecs, 16)
            for t in range(4):
                src = a["ctx"] if t < TT else a["x"]
                act.dma_start(xin[:, t], src[0, (t % TT) * P:(t % TT + 1) * P, :]).then_inc(s_x, 16)
            for n, name in enumerate(("ssm_a_re", "ssm_a_im")):
                for d in range(2):
                    act.dma_start(par_in[0:G, n, d * NS:(d + 1) * NS], a[name][0, d]).then_inc(s_params, 16)
            for d in range(2):
                act.dma_start(par[d * NS:(d + 1) * NS, 0],
                              a["ssm_log_dt"][0, d:d + 1].broadcast_to([NS, G])).then_inc(s_params, 16)
            for n, name in enumerate(("lambda_q1", "lambda_k1", "lambda_q2", "lambda_k2")):
                act.dma_start(lam_in[:, n], a[name][0:1].broadcast_to([P, HD])).then_inc(s_lams, 16)
            with nc.allow_non_contiguous_dma(reason="one word per group and channel, 4 KiB in all"):
                act.dma_start(dskip[:], a["ssm_d"][0].rearrange("(g c) -> c g", c=GC)).then_inc(s_lams, 16)
            for n, name in enumerate(("ssm_b_re", "ssm_b_im")):
                for d in range(2):
                    act.dma_start(braw[d * NS:(d + 1) * NS, n], a[name][0, d].rearrange("g p c -> p g c")
                                  ).then_inc(s_braw, 16)

            act.wait_ge(main_free, 2)
            af(silu_c[:], vcol1[:, 25:57].rearrange("p (s k) -> p k s", s=2), ACT.Silu).then_inc(act_misc, 1)
            for t in range(4):
                act.wait_ge(s_x, 64)
                if t:
                    act.wait_ge(s_ssq, t)
                af(square[:], xin[:, t], ACT.Square, accum_out=ss[:, t:t + 1]).then_inc(s_ssq, 1)
            act.wait_ge(dve_misc, 1)
            af(rstd[:], ss[:], ACT.Sqrt).then_inc(s_sqrt, 1)
            act.wait_ge(dve_misc, 2)
            af(neg_lam[:, 2:4], neg_lam[:, 0:2], ACT.Exp).then_inc(act_misc, 1)
            act.wait_ge(s_sin_in, 1)
            af(par[:, 14:16], par[:, 12:14], ACT.Sin).then_inc(s_sin, 1)

            def h_tile(k):
                for st in range(2):
                    part = xT[:, k, st * L:(st + 1) * L]
                    af(part, part, ACT.Identity, bias=mod1[:, k, 1 - st:2 - st], scale=gain1[:, k, 1 - st:2 - st]
                       ).then_inc(h_ready, 1)
                act.wait_ge(h_ready, 2 * k + 2)
                af(hT[:, :, 0, k, :], xT[:, k, :].rearrange("p (s n) -> p s n", s=2), ACT.Copy).then_inc(h_hi, 1)

            LAND = 256

            def hi(slot, rslot, landed, free):
                act.wait_ge(raw_landed[rslot], landed)
                if free is not None:
                    act.wait_ge(mm_done, free)
                af(wring[:, slot, 0], raw[:, rslot], ACT.Copy).then_inc(hi_done, 1)

            def hi_early(b, it):
                n = it + 1
                free = b * 8 + it
                hi(n % 2, 3 * n % 4, b * 96 + (LAND + 16 * (3 * n // 4 + 1)),
                   None if isinstance(free, int) and free <= 0 else free)

            def mod_copy(b):
                act.wait_ge(ada_cols, b + 2)
                af(modraw[:, ds(b * 8, 8)], ps[:, 4, 0:8], ACT.Copy).then_inc(mod_out, 1)

            act.wait_ge(gains, 1)
            hi(0, 0, LAND + 16, None)
            h_tile(0)
            h_tile(1)
            for b in range(2):
                for it in range(8):
                    if b == 0 and it < 7:
                        h_tile(2 * it + 2)
                        h_tile(2 * it + 3)
                    hi_early(b, it)
                act.wait_ge(mm_done, 8 * b + 8)
                mod_copy(b)
                for c in range(4):
                    af(uT[:, 4 * b + c], ps[:, c, :], ACT.Copy).then_inc(main_free, 1)
            with act.Fori(0, 2) as i:
                for it in range(8):
                    hi_early(i * 2 + 2, it)
                    if it % 2 == 0:
                        act.wait_ge(uv_mm, i * 4 + (it // 2 + 1))
                        af(uv[0:64].rearrange("p g s c -> p s g c"),
                           ps[0:64, 5:7, :].rearrange("p a (b g c) -> p (a b) g c", b=4, g=8), ACT.Copy
                           ).then_inc(uv_out, 1)
                    else:
                        act.wait_ge(u_mm, i * 4 + (it // 2 + 1))
                        af(u[:, ds(i * 32 + 8 * (it // 2), 8), :], ps[:, 7, :].rearrange("p (g n) -> p g n", g=8),
                           ACT.Copy).then_inc(u_out, 1)
                act.wait_ge(mm_done, i * 16 + (M_KV + 8))
                mod_copy(i * 2 + 2)
                for t in range(4):
                    af(kraw[:, t], ps[:, t, :], ACT.Copy).then_inc(main_free, 1)
                for it in range(8):
                    hi_early(i * 2 + 3, it)
                    act.wait_ge(g_mm, i * 8 + (it + 1))
                    af(gt[:], ps[:, 5:7, :].rearrange("p a (b n) -> p a b n", b=4), ACT.Copy).then_inc(g_out, 1)
                    if 2 <= it < 6:
                        t = it - 2
                        act.wait_ge(k_mm, i * 4 + (t + 1))
                        af(kT[:, ds(i * 4, 4), t * P:(t + 1) * P], ps[:, 4, :].rearrange("p (h n) -> p h n", h=4),
                           ACT.Copy).then_inc(kT_out, 1)
                act.wait_ge(mm_done, i * 16 + (M_KV + 16))
                mod_copy(i * 2 + 3)
                for t in range(4):
                    af(kraw[:, t], ps[:, t, :], ACT.Copy).then_inc(main_free, 1)
                act.wait_ge(main_free, i * 8 + 26 + 0)
                act.dma_start(v_spill.rearrange("(t p) n -> p t n", p=P)[:, :, ds(i * NB, NB)], kraw[:]
                              ).then_inc(s_spill, 16)
                act.wait_ge(s_spill, i * 16 + 16)

            def hi_late(m, slot, shift=R_SHIFT2):
                hi(slot, slot, m * 4 + (LAND + 16 + 4 * shift - 4 * slot), 48 if isinstance(m, int) and m < 52 else m - 3)

            def hi_y(n, j):
                hi(j % 4, 2 * j % 4, n * 64 + (LAND + 16 * ((R_GY + 2 * j) // 4 + 1)), n * 8 + (M_GY + j - 3))

            hi_late(M_Q + 1, 1, R_SHIFT1)
            for n in range(2):
                for it in range(8):
                    m = M_Q + 8 * n + it + 2
                    hi_late(m, m % 4, R_SHIFT1)
                    if n and it == 4:
                        act.wait_ge(q_mm, 1)
                        af(qT[:, 0:4, :].rearrange("p h (t n) -> p t h n", t=2),
                           ps[:, 4:6, :].rearrange("p t (h n) -> p t h n", h=4), ACT.Copy).then_inc(qT_out, 1)
                act.wait_ge(mm_done, M_Q + 8 * n + 8)
                if n:
                    act.wait_ge(q_mm, n)
                for t in range(TT):
                    af(qraw[:, t], ps[:, t, :], ACT.Copy).then_inc(main_free, 1)
            act.wait_ge(q_mm, 2)
            af(qT[:, 4:8, :].rearrange("p h (t n) -> p t h n", t=2),
               ps[:, 4:6, :].rearrange("p t (h n) -> p t h n", h=4), ACT.Copy).then_inc(qT_out, 1)

            def probs(qt, un):
                act.wait_ge(s_nm, un + 1)
                for mp in range(2):
                    ins = af(prob[:, qt, mp], ps[:, 2 * qt + mp, :], ACT.Exp, bias=neg_max[:, qt, mp:mp + 1],
                             scale=SCALE, accum_out=row_sum[:, qt, mp:mp + 1])
                ins.then_inc(s_exp, 1)

            def p_out(qt, un):
                act.wait_ge(t_mm, un + 1)
                af(pT[:, qt], ps[:, 4, :].rearrange("p (t n) -> p t n", t=4), ACT.Copy).then_inc(pT_out, 1)

            def gate_out(n, bank):
                act.wait_ge(mm_done, n * 8 + (M_GATE + 8))
                for t in range(TT):
                    if t or not (isinstance(n, int) and n == 0):
                        act.wait_ge(s_gspill, n * 32 + 16 * t)
                    af(gate_st[:], ps[:, bank + t, :], ACT.Sigmoid).then_inc(gate_sig, 1)
                    act.wait_ge(gate_sig, n * 2 + (t + 1))
                    act.dma_start(g_spill[ds(n, 1), t * P:(t + 1) * P, :].squeeze(0), gate_st[:]).then_inc(s_gspill, 16)

            def gate_hi(n, k, last):
                if k < 6 or not last:
                    hi_late(n * 8 + (M_GATE + k + 2), (k + 2) % 4, R_SHIFT1)
                else:
                    hi_y(0, k - 6)

            def att(n, hh, last):
                un = n * 4 + 2 * hh
                probs(1, un + 1)
                gate_hi(n, 4 * hh, last)
                p_out(0, un)
                gate_hi(n, 4 * hh + 1, last)
                if not (last and hh):
                    probs(0, un + 2)
                gate_hi(n, 4 * hh + 2, last)
                p_out(1, un + 1)
                gate_hi(n, 4 * hh + 3, last)

            probs(0, 0)
            att(0, 0, False)
            att(0, 1, False)
            gate_out(0, 6)
            with act.Fori(1, H // 2 - 1) as n:
                att(n, 0, False)
                att(n, 1, False)
                gate_out(n, 6)
            att(H // 2 - 1, 0, True)
            att(H // 2 - 1, 1, True)
            gate_out(H // 2 - 1, 6)
            act.wait_ge(o_ss, 1)
            af(oss[:], oss[:], ACT.Sqrt).then_inc(o_root, 1)
            for n in range(4):
                act.wait_ge(oT_mm, n + 1)
                af(oT[:, 0, 2 * n:2 * n + 2, :], ps[:, 4 + n, :].rearrange("p (h n) -> p h n", h=2), ACT.Copy,
                   scale=gsub[:, 0:1]).then_inc(oT_hi, 1)

            def strip_copy(s, q):
                act.wait_ge(st_mm, q + 1)
                af(strip[:, s].rearrange("p (b g) n -> p b g n", b=2),
                   ps[0:GC, 6:8, 0:480].rearrange("p b (g n) -> p b g n", g=2), ACT.Copy).then_inc(st_out, 1)

            def yj_copy(s, q, i, first):
                act.wait_ge(y_mm, q + 1)
                if not first:
                    act.wait_ge(yT_mm, i)
                af(yj[:, :, s * 64:(s + 1) * 64].rearrange("p t (g c) -> p g t c", g=4),
                   ps[0:NCH, 4 + s, :].rearrange("p (g t c) -> p g t c", g=4, t=CH), ACT.Copy).then_inc(yj_out, 1)

            def gelu(i, ct):
                act.wait_ge(yT_mm, i)
                af(z[:, ds(ct, 1), :].rearrange("p o (j t) -> p (o j) t", t=CH),
                   ps[:, 0, 0:L].rearrange("p (t j) -> p j t", t=CH), ACT.Gelu_apprx_tanh).then_inc(z_out, 1)

            def spread_strip(s, q):
                act.wait_ge(st_done, q + 1)
                for t in range(CH):
                    act.dma_start(toep[t * GC:(t + 1) * GC, s],
                                  strip[:, s, :, (CH - 1 - t) * GC:(CH - 1 - t) * GC + P]).then_inc(s_toep[s], 16)

            def y_quad(u, j, first, last, last_unit):
                i, s = u * 2 + j // 2, j % 2
                q = u * 4 + j
                if not last:
                    strip_copy(1 - s, q + 1)
                if s == 0 and not first:
                    gelu(i, i - 1)

                def ahead(k):
                    if k + 2 < 8:
                        hi_y(u, k + 2)
                    elif not last_unit:
                        hi_y(u + 1, k - 6)
                    else:
                        hi_late(M_GLU + k - 6, k - 6)

                ahead(2 * j)
                if not last:
                    spread_strip(1 - s, q + 1)
                yj_copy(s, q, i, isinstance(u, int) and i == 0)
                ahead(2 * j + 1)

            def y_unit(u, first, last):
                for j in range(4):
                    y_quad(u, j, first and j == 0, last and j == 3, last)
                gate_out(u + 4, 2)
                act.wait_ge(ada_cols, u + 8)
                af(modraw[:, ds(u * 4 + 48, 4)], ps[:, 1, 0:4], ACT.Copy).then_inc(mod_out, 1)

            strip_copy(0, 0)
            spread_strip(0, 0)
            y_unit(0, True, False)
            with act.Fori(1, 3) as unit:
                y_unit(unit, False, False)
            y_unit(3, False, True)
            gelu(8, 7)

            act.wait_ge(z_out, 8)
            af(zs[:, 0], z[:], ACT.Copy).then_inc(zs_hi, 1)
            for n in range(4):
                act.wait_ge(row_mm, n + 1)
                af(g1row[:, n * NB:(n + 1) * NB], ps[:, 4 + n, :], ACT.Copy).then_inc(row_out, 1)
            for b in range(2):
                for it in range(4):
                    m = M_GLU + 4 * b + it + 2
                    hi_late(m, m % 4)
                act.wait_ge(mm_done, M_GLU + 4 * b + 4)
                if b:
                    act.wait_ge(glu_y, 4)
                for c in range(4):
                    af(sig[:, c], ps[:, 4 * b + c, 0:L], ACT.Sigmoid,
                       bias=vcol1[:, 16 + 4 * b + c:17 + 4 * b + c]).then_inc(glu_sig, 1)
                act.wait_ge(glu_y, 4 * b + 4)
                af(ys[:, 0, 4 * b:4 * b + 4], y32[:], ACT.Copy).then_inc(ys_hi, 1)

            def turn_hi(n, b):
                act.wait_ge(mt_mm, n)
                af(mT[:, 0, ds(b * 4, 4), :], ps[:, 0:2, :].rearrange("p a (c n) -> p (a c) n", c=2), ACT.Copy
                   ).then_inc(mt_hi, 1)

            def merge(b, first):
                for it in range(8):
                    hi_late(b * 8 + (M_MERGE + it + 2), (it + 2) % 4)
                    if it == 3 and not first:
                        turn_hi(b, b - 1)

            merge(0, True)
            with act.Fori(1, 4) as b:
                merge(b, False)
            turn_hi(4, 3)

            with act.Fori(0, 4) as b:
                for it in range(8):
                    hi_late(b * 8 + (M_WO + it + 2), (it + 2) % 4)
            for n in range(4):
                act.wait_ge(row_mm, 5 + n)
                af(g2row[:, n * NB:(n + 1) * NB], ps[:, 4 + n, :], ACT.Copy).then_inc(row_out, 1)
            for t in range(TT):
                act.wait_ge(wo_out, 8)
                if t:
                    act.wait_ge(s_ssq, 4 + t)
                af(square2[:], x[:, t], ACT.Square, accum_out=ss[:, t:t + 1]).then_inc(s_ssq, 1)
            act.wait_ge(dve_misc, 3)
            af(rstd[:, 0:2], ss[:, 0:2], ACT.Sqrt).then_inc(s_sqrt, 1)
            for n in range(4):
                act.wait_ge(h32_done, 4 * n + 4)
                af(h2T[:, 0, 4 * n:4 * n + 4], h32[:, 4 * n:4 * n + 4], ACT.Copy).then_inc(h2_hi, 1)

            def at_turn(n, j):
                act.wait_ge(at_mm, n)
                af(actT[:, 0, ds(j * 4, 4), :], ps[:, 4:6, :].rearrange("p a (c n) -> p (a c) n", c=2), ACT.Copy
                   ).then_inc(at_hi, 1)

            def ffn_in(j, first):
                for n in range(16):
                    hi_late(j * 16 + (M_FI + n + 2), (n + 2) % 4)
                    if n == 3 and not first:
                        at_turn(j, j - 1)
                    if n == 7:
                        if not first:
                            act.wait_ge(act_done, j)
                        act.wait_ge(mm_done, j * 16 + (M_FI + 8))
                        for t in range(TT):
                            af(silu_g[:, t], ps[:, t, :], ACT.Silu).then_inc(silu_out, 1)

            ffn_in(0, True)
            with act.Fori(1, FB) as j:
                ffn_in(j, False)
            at_turn(FB, FB - 1)

            with act.Fori(0, FB - 1) as j:
                for n in range(8):
                    hi_late(j * 8 + (M_FO + n + 2), (n + 2) % 4)
            for n in range(6):
                m = M_FO + 8 * (FB - 1) + n + 2
                hi_late(m, m % 4)
            for t in range(TT):
                act.wait_ge(ff_out, 8)
                if t:
                    act.wait_ge(s_ssq, 6 + t)
                af(square3[:], x[:, t], ACT.Square, accum_out=ss[:, t:t + 1]).then_inc(s_ssq, 1)
            act.wait_ge(dve_misc, 4)
            af(rstd[:, 0:2], ss[:, 0:2], ACT.Sqrt).then_inc(s_sqrt, 1)

        @block.vector
        def _(dve):
            V = nc.vector
            seq = Tally(dve_seq)

            def link(ins):
                seq.tick(ins)
                seq.wait(dve)
                return ins

            tt, ts, stt, cp = V.tensor_tensor, V.tensor_scalar, V.scalar_tensor_tensor, V.tensor_copy

            link(V.memset(ones[:], 1.0))
            dve.wait_ge(pe_misc, 1)
            cp(vcol[:], ps[:, 0, 0:112]).then_inc(main_free, 1)
            dve.wait_ge(pe_misc, 2)
            cp(vcol1[:], ps[:, 1, 0:57]).then_inc(main_free, 1)

            LDT, ARE, AIM, XR, TH, N, T0, Q0, SC, DT, ER, MAG, SA, CA, SIN, COS = range(16)
            W = [par[:, n] for n in range(24)]
            dve.wait_ge(s_params, 96)
            dve.wait_ge(pe_misc, 3)
            cp(W[ARE], ps[:, 7, 0:G])
            cp(W[AIM], ps[:, 7, G:2 * G]).then_inc(e_out, 1)
            dve.wait_ge(e_out, 1)

            def exp_of(dst, src):
                link(ts(W[T0], src, 88.8, -104.0, ALU.min, ALU.max))
                link(ts(W[N], W[T0], 1.4426950408889634, ROUND, ALU.mult, ALU.add))
                link(ts(W[N], W[N], -ROUND, None, ALU.add))
                link(stt(W[T0], W[N], -LN2_PARTS[0], W[T0], ALU.mult, ALU.add))
                link(stt(W[T0], W[N], -LN2_PARTS[1], W[T0], ALU.mult, ALU.add))
                link(ts(W[Q0], W[T0], EXP_TAYLOR[0], None, ALU.mult))
                for c in EXP_TAYLOR[1:]:
                    link(stt(W[Q0], W[Q0], c, W[T0], ALU.add, ALU.mult))
                link(ts(W[N], W[N], -127.0, 128.0, ALU.max, ALU.min))
                link(ts(W[N], W[N], 127.0, 8388608.0, ALU.add, ALU.mult))
                link(cp(par_i[:], W[N]))
                link(stt(dst, W[Q0], 1.0, par_i[:].bitcast(F32), ALU.add, ALU.mult))

            exp_of(W[DT], W[LDT])
            tt(W[XR], W[ARE], W[DT], ALU.mult)
            link(tt(W[TH], W[AIM], W[DT], ALU.mult))
            exp_of(W[ER], W[XR])
            link(ts(W[N], W[TH], 0.15915494309189535, ROUND, ALU.mult, ALU.add))
            link(ts(W[N], W[N], -ROUND, None, ALU.add))
            for part in TWO_PI_PARTS:
                link(stt(W[TH], W[N], -part, W[TH], ALU.mult, ALU.add))
            link(ts(W[SA], W[TH], 3.1415925, -3.1415925, ALU.min, ALU.max))
            link(stt(W[T0], W[SA], -1.0, W[SA], ALU.mult, ALU.max))
            ts(W[CA], W[T0], -1.0, 1.5707963267948966, ALU.mult, ALU.add).then_inc(s_sin_in, 1)

            dve.wait_ge(s_ssq, 4)
            ts(ss[:], ss[:], 1.0 / D, EPS, ALU.mult, ALU.add).then_inc(dve_misc, 1)
            dve.wait_ge(s_lams, 80)
            lq = lam_in[:].rearrange("p (s w) n -> p s w n", w=2)
            link(tt(lam_pr[:], lq[:, :, 0], lq[:, :, 1], ALU.mult))
            V.reduce_sum(neg_lam[:, 0:2], lam_pr[:], AX_X).then_inc(dve_misc, 1)
            dve.wait_ge(s_sqrt, 1)
            link(V.reciprocal(rstd[:], rstd[:]))
            for t in range(4):
                ts(xin[:, t], xin[:, t], rstd[:, t:t + 1], None, ALU.mult).then_inc(x2_done, 1)

            dve.wait_ge(s_sin, 1)
            link(tt(lam_t[:, 0], W[ER], W[COS], ALU.mult))
            link(tt(lam_t[:, 2], W[ER], W[SIN], ALU.mult))
            link(ts(lam_t[:, 1], lam_t[:, 2], -1.0, None, ALU.mult))
            FR, FI, DEN, T1, T2, T3 = (W[n] for n in range(16, 22))
            link(tt(T1, W[ARE], W[ARE], ALU.mult))
            link(tt(T2, W[AIM], W[AIM], ALU.mult))
            link(tt(T1, T1, T2, ALU.add))
            link(V.reciprocal(DEN, T1))
            link(ts(T1, lam_t[:, 0], -1.0, None, ALU.add))
            link(tt(T2, T1, W[ARE], ALU.mult))
            link(tt(T3, lam_t[:, 2], W[AIM], ALU.mult))
            link(tt(T2, T2, T3, ALU.add))
            link(tt(FR, T2, DEN, ALU.mult))
            link(tt(T2, lam_t[:, 2], W[ARE], ALU.mult))
            link(tt(T3, T1, W[AIM], ALU.mult))
            link(tt(T2, T2, T3, ALU.subtract))
            link(tt(FI, T2, DEN, ALU.mult))
            dve.wait_ge(s_braw, 64)

            def wide(col):
                return col.unsqueeze(2).broadcast_to([P, G, GC])

            link(tt(bbar[:, 0], braw[:, 0], wide(FR), ALU.mult))
            link(tt(btmp[:], braw[:, 1], wide(FI), ALU.mult))
            link(tt(bbar[:, 0], bbar[:, 0], btmp[:], ALU.subtract))
            link(tt(bbar[:, 1], braw[:, 1], wide(FR), ALU.mult))
            link(tt(btmp[:], braw[:, 0], wide(FI), ALU.mult))
            link(tt(bbar[:, 1], bbar[:, 1], btmp[:], ALU.add))

            def power(dst, n, one, other):
                def rep(x):
                    return x.unsqueeze(1).broadcast_to([P, n, G])
                tmp = btmp[:].rearrange("p g c -> p (g c)")[:, 0:n * G].rearrange("p (n g) -> p n g", n=n)
                re, im = pw[:, one, 0], pw[:, one, 1]
                ore, oim = pw[:, other:other + n, 0], pw[:, other:other + n, 1]
                link(tt(pw[:, dst:dst + n, 0], ore, rep(re), ALU.mult))
                link(tt(tmp, oim, rep(im), ALU.mult))
                link(tt(pw[:, dst:dst + n, 0], pw[:, dst:dst + n, 0], tmp, ALU.subtract))
                link(tt(pw[:, dst:dst + n, 1], oim, rep(re), ALU.mult))
                link(tt(tmp, ore, rep(im), ALU.mult))
                link(tt(pw[:, dst:dst + n, 1], pw[:, dst:dst + n, 1], tmp, ALU.add))

            V.memset(pw[:, 0, 0], 1.0)
            V.memset(pw[:, 0, 1], 0.0)
            cp(pw[:, 1, 0], lam_t[:, 0])
            link(cp(pw[:, 1, 1], lam_t[:, 2]))
            power(2, 1, 1, 1)
            power(3, 2, 2, 1)
            power(5, 4, 4, 1)
            cp(lam8_t[:, 0], pw[:, 8, 0])
            ts(lam8_t[:, 1], pw[:, 8, 1], -1.0, None, ALU.mult)
            cp(lam8_t[:, 2], pw[:, 8, 1])
            for c in range(2):
                cp(tab[0:NS, c], pw[0:NS, 0:CH, c, :].rearrange("p i g -> p g i")[:, :, ::-1])
                ins = cp(tab[NS:, c], pw[NS:, 0:CH, c, :].rearrange("p i g -> p g i"))
            ins.then_inc(tab_done, 1)
            dve.wait_ge(act_misc, 2)
            link(tt(neg_lam[:, 0:1], neg_lam[:, 3:4], neg_lam[:, 2:3], ALU.subtract))
            link(ts(neg_lam[:, 0:1], neg_lam[:, 0:1], -LAM_INIT, None, ALU.add))
            link(ts(gsub[:], vcol1[:, 24:25], 1.0 - LAM_INIT, None, ALU.mult))

            def ada_row(i, s, n):
                dve.wait_ge(ada_used, n * 8 + 8)
                cp(mod_row[0:2, ds(n * NB, NB)], ps[0:2, s, :]).then_inc(main_free, 1)

            with dve.Fori(0, 2) as i:
                for s in range(2):
                    ada_row(i, s, i * 2 + s)
            with dve.Fori(0, KT // 2) as i:
                for s in range(2):
                    dve.wait_ge(xT_mm, i * 2 + (s + 1))
                    cp(xT[:, ds(i * 2 + s, 1), :].squeeze(1), ps[:, 4 + s, :]).then_inc(xT_out, 1)
            with dve.Fori(2, 4) as i:
                for s in range(2):
                    ada_row(i, s, i * 2 + s)
            dve.wait_ge(ada_cols, 1)
            link(tt(mod1[:], ps[:, 6, 0:64].rearrange("p (j s) -> p j s", s=2),
                    vcol[:, 0:32].unsqueeze(2).broadcast_to([P, 32, 2]), ALU.add))
            dve.wait_ge(xT_out, KT)
            stt(gain1[:], mod1[:, KT:2 * KT, :], 1.0, vcol[:, 96:112].unsqueeze(2).broadcast_to([P, KT, 2]),
                ALU.add, ALU.mult).then_inc(gains, 1)

            LAND = 256

            def lo(m, slot, rslot):
                dve.wait_ge(hi_done, m + 1)
                tt(wring[:, slot, 1], raw[:, rslot], wring[:, slot, 0].bitcast(F32), ALU.subtract).then_inc(lo_done, 1)

            def ada_sum(b, t):
                pos = 3 * (t // 2) + 1 + t % 2
                dve.wait_ge(raw_landed[pos % 4], b * 96 + (LAND + 16 * (pos // 4 + 1)))
                dst = acc[:, t // 8]
                for k in range(2):
                    col = silu_c[:, 2 * (t % 8) + k, 0:1]
                    if t % 8 == 0 and k == 0:
                        dve.wait_ge(ada_cols, b + 1)
                        link(ts(dst, raw[:, pos % 4, 0], col, None, ALU.mult))
                        continue
                    if k == 0:
                        dve.wait_ge(ada2_used, b * 16 + t)
                    ins = stt(dst, raw[:, pos % 4, k], col, dst, ALU.mult, ALU.add)
                    if k:
                        ins.then_inc(ada2_used, 1)
                    else:
                        link(ins)

            def ada_lo(b, it):
                ada_sum(b, 2 * it)
                ada_sum(b, 2 * it + 1)
                lo(b * 8 + (it + 1), (it + 1) % 2, 3 * (it + 1) % 4)

            def rope_in_place(xt, t, signal):
                xv = xt.rearrange("p (h e) -> p h e", h=8)
                xf = xt.rearrange("p (h a f e) -> p h a f e", h=8, a=2, f=2)
                hf = half_t[:].rearrange("p (h a f e) -> p h a f e", h=8, a=2, f=2)
                sf = rope[:, t, 1].rearrange("p (a f e) -> p a f e", a=2, f=2)
                for f in range(2):
                    link(tt(hf[:, :, :, f], xf[:, :, :, 1 - f], sf[:, :, f].unsqueeze(1).broadcast_to([P, 8, 2, 16]),
                            ALU.mult))
                link(tt(xv, xv, rope[:, t, 0].unsqueeze(1).broadcast_to([P, 8, HD]), ALU.mult))
                ins = tt(xt, xt, half_t[:], ALU.add)
                if signal is None:
                    link(ins)
                else:
                    ins.then_inc(signal, 1)

            def h_low(k):
                dve.wait_ge(h_hi, k + 1)
                tt(hT[:, :, 1, k, :], xT[:, k, :].rearrange("p (s n) -> p s n", s=2), hT[:, :, 0, k, :].bitcast(F32),
                   ALU.subtract).then_inc(h_lo, 1)

            lo(0, 0, 0)
            h_low(0)
            h_low(1)
            for b in range(2):
                for it in range(8):
                    if b == 0 and it < 7:
                        h_low(2 * it + 2)
                        h_low(2 * it + 3)
                    ada_lo(b, it)
            with repeat(dve, 0, 2, {seq: 32 + 7 + 16}) as i:
                for it in range(8):
                    if it % 2 == 0:
                        dve.wait_ge(main_free, 18)
                        if it:
                            dve.wait_ge(uv_mm, i * 4 + it // 2)
                        cp(u_s[:], uT[:, ds(i * 4 + it // 2, 1), :].rearrange("p o (j s) -> p (o s) j", s=CH)
                           ).then_inc(u_sorted, 1)
                    ada_lo(i * 2 + 2, it)
                for it in range(8):
                    if it == 0:
                        dve.wait_ge(main_free, i * 8 + 22)
                        rope_in_place(kraw[:, 2], 0, None)
                    if it == 1:
                        rope_in_place(kraw[:, 3], 1, k_rot)
                    ada_lo(i * 2 + 3, it)
                    dve.wait_ge(e_mm, i * 8 + (it + 1))
                    src = ps[:, 7, :].rearrange("p (c g j) -> p c g j", c=2, g=4)
                    gsl = ds(i * 32 + 4 * it, 4)
                    dst = ustate[0:NS, :, :, gsl].rearrange("p k c g -> p c g k")
                    seq.tick(cp(dst, src[0:NS]))
                    for half in range(2):
                        dst = ustate[NS:, half * NCH:(half + 1) * NCH, :, gsl].rearrange("p k c g -> p c g k")
                        ins = cp(dst, src[NS:, :, :, half * NCH:(half + 1) * NCH][:, :, :, ::-1])
                        if half:
                            ins.then_inc(e_out, 1)
                        else:
                            seq.tick(ins)

            def lo_late(m, slot):
                lo(m, slot, slot)

            lo_late(M_Q + 1, 1)
            for n in range(2):
                for it in range(8):
                    m = M_Q + 8 * n + it + 2
                    lo_late(m, m % 4)
                    if n and it == 1:
                        dve.wait_ge(main_free, 36)
                        rope_in_place(qraw[:, 0], 0, None)
                        rope_in_place(qraw[:, 1], 1, q_rot)
            dve.wait_ge(main_free, 38)
            rope_in_place(qraw[:, 0], 0, None)
            rope_in_place(qraw[:, 1], 1, q_rot)
            dve.wait_ge(mod_out, 6)
            link(tt(modc[:, 0:48], modraw[:, 0:48], vcol[:, 32:80], ALU.add))
            link(stt(gain2[:], modc[:, 32:48], 1.0, vcol1[:, 0:16], ALU.add, ALU.mult))

            def top(qt, un):
                dve.wait_ge(s_mm, un + 1)
                link(V.reduce_max(row_max[:, qt], ps[:, 2 * qt:2 * qt + 2, :], AX_X))
                ts(neg_max[:, qt], row_max[:, qt], -SCALE, None, ALU.mult).then_inc(s_nm, 1)

            def combine(qt, un):
                dve.wait_ge(s_exp, un + 1)
                link(V.reciprocal(row_inv[:, qt], row_sum[:, qt]))
                link(tt(row_inv[:, qt, 1:2], row_inv[:, qt, 1:2], neg_lam[:, 0:1], ALU.mult))
                first_map = prob[:, qt, 0]
                link(ts(first_map, first_map, row_inv[:, qt, 0:1], None, ALU.mult))
                stt(first_map, prob[:, qt, 1], row_inv[:, qt, 1:2], first_map, ALU.mult, ALU.add).then_inc(s_pd, 1)

            def head_out(qt, hd, un):
                dve.wait_ge(o_mm, un + 1)
                ts(o_all[:, ds(hd, 1), qt, :].squeeze(1), ps[:, 5, qt * P:(qt + 1) * P], 1.0, None, ALU.mult
                   ).then_inc(o_out, 1)

            def att(n, hh, first, last):
                hd = n * 2 + hh

                def ahead(k):
                    if k < 6 or not last:
                        lo_late(n * 8 + (M_GATE + k + 2), (k + 2) % 4)
                    else:
                        lo(M_GY + k - 6, k - 6, 2 * (k - 6))

                top(1, hd * 2 + 1)
                if not (last and hh):
                    queries(hd + 1)
                ahead(4 * hh)
                combine(0, hd * 2)
                if not first:
                    head_out(1, hd - 1, hd * 2 - 1)
                ahead(4 * hh + 1)
                if not (last and hh):
                    top(0, hd * 2 + 2)
                ahead(4 * hh + 2)
                combine(1, hd * 2 + 1)
                head_out(0, hd, hd * 2)
                ahead(4 * hh + 3)

            def queries(hd):
                seq.tick(cp(qh[0:HD, 0], qT[0:HD, ds(hd, 1), :].squeeze(1)))
                cp(qh[HD:, 1], qT[HD:, ds(hd, 1), :].squeeze(1)).then_inc(qh_in, 1)

            link(V.memset(qh[:], 0.0))
            dve.wait_ge(qT_out, 2)
            queries(0)
            top(0, 0)
            att(0, 0, True, False)
            att(0, 1, False, False)
            with repeat(dve, 1, H // 2 - 1, {seq: 18}) as n:
                att(n, 0, False, False)
                att(n, 1, False, False)
            att(H // 2 - 1, 0, False, True)
            att(H // 2 - 1, 1, False, True)
            head_out(1, H - 1, 2 * H - 1)
            dve.wait_ge(o_out, 2 * H)
            o_rows = o_all[:].rearrange("p h q e -> p (h q) e")
            link(tt(osq[:], o_rows, o_rows, ALU.mult))
            link(V.reduce_sum(oss[:], osq[:], AX_X))
            ts(oss[:], oss[:], 1.0 / P, EPS, ALU.mult, ALU.add).then_inc(o_ss, 1)
            dve.wait_ge(o_root, 1)
            link(V.reciprocal(oss[:], oss[:]))
            tt(o_rows, o_rows, oss[:].unsqueeze(2).broadcast_to([P, 2 * H, P]), ALU.mult).then_inc(o_norm, 1)
            for n in range(4):
                dve.wait_ge(oT_hi, n + 1)
                stt(oT[:, 1, 2 * n:2 * n + 2, :], ps[:, 4 + n, :].rearrange("p (h n) -> p h n", h=2), gsub[:, 0:1],
                    oT[:, 0, 2 * n:2 * n + 2, :].bitcast(F32), ALU.mult, ALU.subtract).then_inc(oT_lo, 1)

            dve.wait_ge(scanned, 1)
            for n in range(2):
                dve.wait_ge(c_mm, n + 1)
                for b in range(2):
                    ins = ts(cT[:, n, 32 * b:32 * b + 32, :].rearrange("p g c -> p (g c)"), ps[:, 2 * n + b, :],
                             -1.0 if n else 1.0, None, ALU.mult)
                ins.then_inc(c_out, 1)

            def strip_in(s, q, first):
                dve.wait_ge(r_built, q + 1)
                seq.wait(dve)
                if not first:
                    dve.wait_ge(st_mm, q)
                r = rmat[:, s].rearrange("p c g t e -> p (c g) (t e)")
                st = strip_r[:].rearrange("p c g b e -> p (c g) (b e)")
                seq.tick(cp(bquad[:, s], bbar[:, :, ds(q * 4, 4), :]))
                seq.tick(cp(st[0:NS, :, 7 * GC:], r[0:NS]))
                cp(st[NS:, :, 0:8 * GC], r[NS:]).then_inc(sr_done, 1)

            def skip_in(s, q):
                dve.wait_ge(st_out, q + 1)
                link(tt(dblk[:], ident[0:GC, 0:GC].unsqueeze(1).broadcast_to([GC, 4, GC]),
                        dskip[:, ds(q * 4, 4)].unsqueeze(2).broadcast_to([GC, 4, GC]), ALU.mult))
                mid = strip[:, s, :, 7 * GC:8 * GC]
                tt(mid, mid, dblk[:], ALU.add).then_inc(st_done, 1)

            def states_in(s, q):
                gsl = ds(q * 4, 4)
                if not (isinstance(q, int) and q == 0):
                    dve.wait_ge(hq_done, q)
                seq.tick(cp(uquad[:, s], u[:, gsl, NCH:]))
                seq.tick(cp(hq_raw[0:NS], ustate[0:NS, NCH - 1:2 * NCH - 1, :, gsl].rearrange("p k c g -> p c g k")))
                link(cp(hq_raw[NS:, :, :, ::-1], ustate[NS:, NCH - 1:2 * NCH - 1, :, gsl].rearrange("p k c g -> p c g k")))

                def lam(rows, n):
                    return lam_t[:, rows, gsl].unsqueeze(3).broadcast_to([P, n, 4, NCH])
                seq.tick(tt(hq_t[:], hq_raw[:, ::-1], lam(slice(1, 3), 2), ALU.mult))
                for c in range(2):
                    ins = tt(hq[:, s, c], hq_raw[:, c], lam_t[:, 0, gsl].unsqueeze(2).broadcast_to([P, 4, NCH]), ALU.mult)
                    if c:
                        link(ins)
                    else:
                        seq.tick(ins)
                tt(hq[:, s], hq[:, s], hq_t[:], ALU.add).then_inc(hq_done, 1)

            def r_imag(s, q, free):
                if free is not None:
                    dve.wait_ge(y_mm, free)
                T, C, tmp = r_parts(s, q, rtmp[1])
                o = rmat[:, s, 1, :, ::-1]
                seq.tick(tt(o, C[1], T[0], ALU.mult))
                link(tt(tmp, C[0], T[1], ALU.mult))
                link(tt(o, o, tmp, ALU.subtract))

            def g2_sum(u, t):
                pos = 2 * t + 1
                dve.wait_ge(raw_landed[pos % 4], u * 64 + (LAND + 16 * ((R_GY + pos) // 4 + 1)))
                for k in range(2):
                    col = silu_c[:, 2 * t + k, 0:1]
                    if t == 0 and k == 0:
                        dve.wait_ge(ada_cols, u + 7)
                        link(ts(acc2[:], raw[:, pos % 4, 0], col, None, ALU.mult))
                        continue
                    if k == 0:
                        dve.wait_ge(ada2_used, u * 8 + (96 + t))
                    ins = stt(acc2[:], raw[:, pos % 4, k], col, acc2[:], ALU.mult, ALU.add)
                    if k:
                        ins.then_inc(ada2_used, 1)
                    else:
                        link(ins)

            def y_quad(u, j, last, before_last, last_unit):
                s = j % 2
                q = u * 4 + j

                def ahead(k):
                    g2_sum(u, k)
                    if k + 2 < 8:
                        lo(u * 8 + (M_GY + k + 2), (k + 2) % 4, 2 * (k + 2) % 4)
                    elif not last_unit:
                        lo(u * 8 + (M_GY + k + 2), (k + 2) % 4, 2 * (k - 6) % 4)
                    else:
                        lo_late(M_GLU + k - 6, k - 6)

                if not last:
                    skip_in(1 - s, q + 1)
                    states_in(1 - s, q + 1)
                if not before_last:
                    r_imag(s, q + 2, q + 1)
                ahead(2 * j)
                if not before_last:
                    strip_in(s, q + 2, False)
                ahead(2 * j + 1)

            def y_unit(u, last):
                for j in range(4):
                    y_quad(u, j, last and j == 3, last and j >= 2, last)

            dve.wait_ge(c_out, 2)
            r_imag(0, 0, None)
            r_imag(1, 1, None)
            dve.wait_ge(scanned, 2)
            strip_in(0, 0, True)
            skip_in(0, 0)
            states_in(0, 0)
            strip_in(1, 1, False)
            with repeat(dve, 0, 3, {seq: 4 * 14}) as unit:
                y_unit(unit, False)
            y_unit(3, True)
            dve.wait_ge(mod_out, 10)
            link(tt(modc[:, 48:64], modraw[:, 48:64], vcol[:, 80:96], ALU.add))

            def diagonals(dst, first, n):
                return tt(dst, ident[:].unsqueeze(1).broadcast_to([P, n, P]),
                          modc[:, first:first + n].unsqueeze(2).broadcast_to([P, n, P]), ALU.mult)

            dve.wait_ge(y_mm, NQ)
            diagonals(diag[:], 0, 16).then_inc(diag_done, 1)
            dve.wait_ge(zs_hi, 1)
            tt(zs[:, 1], z[:], zs[:, 0].bitcast(F32), ALU.subtract).then_inc(zs_lo, 1)
            for b in range(2):
                for it in range(4):
                    m = M_GLU + 4 * b + it + 2
                    lo_late(m, m % 4)
                if b:
                    dve.wait_ge(ys_lo, 1)
                for c in range(4):
                    dve.wait_ge(glu_sig, 4 * b + c + 1)
                    tt(y32[:, c], z[:, 4 * b + c], sig[:, c], ALU.mult).then_inc(glu_y, 1)
                dve.wait_ge(ys_hi, b + 1)
                tt(ys[:, 1, 4 * b:4 * b + 4], y32[:], ys[:, 0, 4 * b:4 * b + 4].bitcast(F32), ALU.subtract
                   ).then_inc(ys_lo, 1)

            def turn_lo(n, b):
                dve.wait_ge(mt_hi, n)
                tt(mT[:, 1, ds(b * 4, 4), :], ps[:, 0:2, :].rearrange("p a (c n) -> p (a c) n", c=2),
                   mT[:, 0, ds(b * 4, 4), :].bitcast(F32), ALU.subtract).then_inc(mt_lo, 1)

            def merge(b, first):
                for it in range(8):
                    lo_late(b * 8 + (M_MERGE + it + 2), (it + 2) % 4)
                    if it == 3 and not first:
                        turn_lo(b, b - 1)
                    if it == 4:
                        dve.wait_ge(s_gates, b * 32 + 32)
                        dve.wait_ge(mm_done, b * 8 + (M_MERGE + 4))
                        tt(m_ssm[:], ps[:, 4:6, :], gates[:, ds(b, 1), 0].squeeze(1), ALU.mult).then_inc(ms_done, 1)
                dve.wait_ge(mm_done, b * 8 + (M_MERGE + 8))
                link(tt(merged[:], ps[:, 6:8, :], gates[:, ds(b, 1), 1].squeeze(1), ALU.mult))
                dve.wait_ge(ms_done, b + 1)
                tt(merged[:], merged[:], m_ssm[:], ALU.add).then_inc(m_done, 1)

            merge(0, True)
            with repeat(dve, 1, 4, {seq: 1}) as b:
                merge(b, False)
            turn_lo(4, 3)

            dve.wait_ge(m_done, 4)
            diagonals(diag2[:], 48, 16).then_inc(diag_done, 1)
            dve.wait_ge(s_xre, 16)
            dve.wait_ge(row_out, 4)

            def out_proj(i):
                for s in range(2):
                    for it in range(8):
                        lo_late(i * 16 + (M_WO + 8 * s + it + 2), (it + 2) % 4)
                    dve.wait_ge(mm_done, i * 16 + (M_WO + 8 * s + 8))
                    for t in range(TT):
                        cols = ds(i * 2 * NB + s * NB, NB)
                        link(tt(gx[:, t], ps[:, 2 * s + t, :], g1row[:, cols], ALU.mult))
                        tt(x[:, t, cols], x[:, t, cols], gx[:, t], ALU.add).then_inc(wo_out, 1)
                    dve.wait_ge(wo_out, i * 4 + (2 * s + 2))

            with repeat(dve, 0, 2, {seq: 4}) as i:
                out_proj(i)

            dve.wait_ge(row_mm, 8)
            dve.wait_ge(s_ssq, 6)
            ts(ss[:, 0:2], ss[:, 0:2], 1.0 / D, EPS, ALU.mult, ALU.add).then_inc(dve_misc, 1)
            dve.wait_ge(s_sqrt, 2)
            link(V.reciprocal(rstd[:, 0:2], rstd[:, 0:2]))
            for t in range(TT):
                ts(x2[:, t], x[:, t], rstd[:, t:t + 1], None, ALU.mult).then_inc(x2_done, 1)
            for k in range(KT):
                dve.wait_ge(x2_mm, k // 2 + 1)
                ts(h32[:, k], ps[:, 4 + (k // 2) % 4, (k % 2) * L:(k % 2 + 1) * L], gain2[:, k:k + 1],
                   modc[:, 16 + k:17 + k], ALU.mult, ALU.add).then_inc(h32_done, 1)
            for n in range(4):
                dve.wait_ge(h2_hi, n + 1)
                tt(h2T[:, 1, 4 * n:4 * n + 4], h32[:, 4 * n:4 * n + 4], h2T[:, 0, 4 * n:4 * n + 4].bitcast(F32),
                   ALU.subtract).then_inc(h2_lo, 1)

            def at_turn(n, j):
                dve.wait_ge(at_hi, n)
                tt(actT[:, 1, ds(j * 4, 4), :], ps[:, 4:6, :].rearrange("p a (c n) -> p (a c) n", c=2),
                   actT[:, 0, ds(j * 4, 4), :].bitcast(F32), ALU.subtract).then_inc(at_lo, 1)

            def ffn_in(j, first):
                for n in range(16):
                    lo_late(j * 16 + (M_FI + n + 2), (n + 2) % 4)
                    if n == 3 and not first:
                        at_turn(j, j - 1)
                dve.wait_ge(silu_out, j * 2 + 2)
                dve.wait_ge(mm_done, j * 16 + (M_FI + 16))
                tt(act32[:], ps[:, 2:4, :], silu_g[:], ALU.mult).then_inc(act_done, 1)

            ffn_in(0, True)
            with dve.Fori(1, FB) as j:
                ffn_in(j, False)
            at_turn(FB, FB - 1)

            def act_to(j, g):
                cp(act_s[:, g], actT[:, :, ds(j * 4 + 2 * g, 2), :].bitcast(F32)).then_inc(act_in, 1)

            def ffn_out(j, last):
                for n in range(6 if last else 8):
                    lo_late(j * 8 + (M_FO + n + 2), (n + 2) % 4)
                    if n in (3, 7) and not last:
                        dve.wait_ge(mm_done, j * 8 + (M_FO + n + 1))
                        act_to(j + 1, n // 4)

            dve.wait_ge(mm_done, M_FO)
            dve.wait_ge(at_lo, FB)
            act_to(0, 0)
            act_to(0, 1)
            with dve.Fori(0, FB - 1) as j:
                ffn_out(j, False)
            ffn_out(FB - 1, True)
            for cb in range(4):
                dve.wait_ge(mm_done, M_FO + 8 * FB - 3 + cb)
                cols = slice(cb * NB, (cb + 1) * NB)
                for t in range(TT):
                    if cb:
                        dve.wait_ge(ff_out, 2 * cb - 1 + t)
                    link(tt(gx_f[:, t], ps[:, 2 * cb + t, :], g2row[:, cols], ALU.mult))
                    tt(x[:, t, cols], x[:, t, cols], gx_f[:, t], ALU.add).then_inc(ff_out, 1)
            dve.wait_ge(s_ssq, 8)
            ts(ss[:, 0:2], ss[:, 0:2], 1.0 / D, EPS, ALU.mult, ALU.add).then_inc(dve_misc, 1)
            dve.wait_ge(s_sqrt, 3)
            link(V.reciprocal(rstd[:, 0:2], rstd[:, 0:2]))
            dve.wait_ge(s_normf, 16)
            for t in range(TT):
                stt(fin[:, t], x[:, t], rstd[:, t:t + 1], normf[:], ALU.mult, ALU.mult).then_inc(f_done, 1)

        @block.gpsimd
        def _(pool):
            pt = nc.gpsimd.tensor_tensor
            seq = Tally(pool_seq)

            def link(ins):
                seq.tick(ins)
                seq.wait(pool)

            def products(out_a, out_b, a1, b1, a2, b2, op_a, a3, b3, a4, b4, op_b, tmps, done):
                for n, (o, p0, p1, p2, p3, op) in enumerate(((out_a, a1, b1, a2, b2, op_a), (out_b, a3, b3, a4, b4, op_b))):
                    seq.tick(pt(o, p0, p1, ALU.mult))
                    tmp = tmps[n]
                    link(pt(tmp, p2, p3, ALU.mult))
                    if n:
                        pt(o, o, tmp, op).then_inc(done, 1)
                    else:
                        seq.tick(pt(o, o, tmp, op))

            pool.wait_ge(tab_done, 1)

            def g_build(i, s, free):
                if free is not None:
                    pool.wait_ge(g_mm, free)
                gsl = ds(i * 8 + 4 * s, 4)
                shape = [P, 4, CH, GC]
                T = [tab[:, c, gsl, :].unsqueeze(3).broadcast_to(shape) for c in range(2)]
                B = [bbar[:, c, gsl, :].unsqueeze(2).broadcast_to(shape) for c in range(2)]
                o = [gp[:, s, c].rearrange("p g (s c) -> p g s c", s=CH) for c in range(2)]
                tmp = [t[:].rearrange("p (g s c) -> p g s c", g=4, s=CH) for t in ptmp]
                products(o[0], o[1], T[0], B[0], T[1], B[1], ALU.subtract, T[0], B[1], T[1], B[0], ALU.add, tmp, g_built)

            for s in range(2):
                g_build(0, s, None)
                pool.wait_ge(g_built, s + 1)
            with repeat(pool, 1, NQ // 2, {seq: 10}) as i:
                for s in range(2):
                    g_build(i, s, i * 2 + (s - 1))
                    pool.wait_ge(g_built, i * 2 + (s + 1))

            pool.wait_ge(e_out, NQ + 1)
            with repeat(pool, 1, 2 * NCH, {seq: 4}) as k:
                h = ustate[:, ds(k - 1, 1), :, :].squeeze(1)
                seq.tick(pt(scan_t[:, 0], h, lam8_t[:, 0].unsqueeze(1).broadcast_to([P, 2, G]), ALU.mult))
                link(pt(scan_t[:, 1, ::-1], h, lam8_t[:, 1:3][:, ::-1], ALU.mult))
                link(pt(scan_t[:, 0], scan_t[:, 0], scan_t[:, 1], ALU.add))
                hk = ustate[:, ds(k, 1), :, :].squeeze(1)
                link(pt(hk, hk, scan_t[:, 0], ALU.add))
            nc.gpsimd.memset(scan_t[:, 0, 0, 0:1], 0.0).then_inc(scanned, 1)
            nc.gpsimd.memset(strip_r[:], 0.0).then_inc(scanned, 1)

            pool.wait_ge(c_out, 2)
            pool.wait_ge(o_norm, 1)

            def r_real(s, q, free):
                if free is not None:
                    pool.wait_ge(y_mm, free)
                T, C, tmp = r_parts(s, q, rtmp[0])
                o = rmat[:, s, 0, :, ::-1]
                seq.tick(pt(o, C[0], T[0], ALU.mult))
                link(pt(tmp, C[1], T[1], ALU.mult))
                pt(o, o, tmp, ALU.add).then_inc(r_built, 1)
                pool.wait_ge(r_built, q + 1)

            for s in range(2):
                r_real(s, s, None)
            with repeat(pool, 1, NQ // 2, {seq: 4}) as i:
                for s in range(2):
                    r_real(s, i * 2 + s, i * 2 + (s - 1))


_INS = ["x", "c", "ctx", "c_ctx", "w_ada", "b_ada", "norm1_g", "w_in", "ssm_a_re", "ssm_a_im", "ssm_log_dt",
        "ssm_b_re", "ssm_b_im", "ssm_c_re", "ssm_c_im", "ssm_d", "w_glu", "b_glu", "lambda_q1", "lambda_k1",
        "lambda_q2", "lambda_k2", "subln_g", "w_proj_ssm", "w_proj_attn", "w_out", "norm2_g", "w_ffn_in",
        "w_ffn_out", "norm_f_g"]


def _rope_table():
    f = np.float32
    pos = np.arange(L)
    inv = (f(1.0) / (f(10000.0) ** (np.arange(0, 32, 2, dtype=f) / f(32)))).astype(f)
    cos, sin = np.empty((L, 2, 2, 16), f), np.empty((L, 2, 2, 16), f)
    for a, p in enumerate((pos // 64, pos % 64)):
        ang = p.astype(f)[:, None] * inv
        cos[:, a, 0] = cos[:, a, 1] = np.cos(ang)
        sin[:, a, 0], sin[:, a, 1] = -np.sin(ang), np.sin(ang)
    return np.stack([cos.reshape(L, HD), sin.reshape(L, HD)], axis=1)


def kernel(**inputs):
    import concourse.bacc as _bacc
    from concourse.bass_utils import run_bass_kernel_spmd as _run

    nc = _bacc.Bacc("TRN2", target_bir_lowering=False, num_devices=1)
    arrays, args = {}, {}
    given = {n: np.ascontiguousarray(inputs[n]) for n in _INS}
    given["ident"] = np.eye(P, dtype=np.float32)
    given["rope"] = _rope_table()
    for name, v in given.items():
        arrays[f"in_{name}_dram"] = v
        args[name] = nc.dram_tensor(f"in_{name}_dram", v.shape, mybir.dt.from_np(v.dtype), kind="ExternalInput").ap()
    out = nc.dram_tensor("out_0_dram", (1, L, D), F32, kind="ExternalOutput").ap()
    layer_program(nc, args, out)
    r = _run(nc, [arrays], core_ids=[0])
    return r.results[0]["out_0_dram"]
```
